# Optimizing a Trainium2 kernel written in Bass

```python
import jax, jax.numpy as jnp
from jax import lax
import numpy as np

D_MODEL = 1024
BATCH = 1
SEQ = 256
DEPTH = 2

MEM_LEN = 256

ATTN_HEADS = 8
ATTN_WIDTH = D_MODEL // 2
ATTN_HEAD_DIM = ATTN_WIDTH // ATTN_HEADS
POOL_GROUPS = 4
POOL_WIDTH = D_MODEL // 4
POOL_GROUP_DIM = POOL_WIDTH // POOL_GROUPS
POOL_WINDOWS = (2, 4, 8, 16)
CONV_GROUPS = 4
CONV_WIDTH = D_MODEL // 4
CONV_K = 3
MIX_WIDTH = ATTN_WIDTH + POOL_WIDTH + CONV_WIDTH
IN_SPLIT_WIDTHS = (ATTN_WIDTH, ATTN_WIDTH, ATTN_WIDTH, POOL_WIDTH, CONV_WIDTH, CONV_WIDTH, CONV_WIDTH)
IN_PROJ_WIDTH = sum(IN_SPLIT_WIDTHS)

DILATED_BRANCHES = ((128, 1), (512, 4), (2048, 16))
MAX_WINDOW = 2048
Q_BLOCK = 128
NEG_INF = -1e30

REL_BUCKETS = 32
REL_MAX_DIST = 128

XATTN_HEADS = 4
XATTN_HEAD_DIM = 128
XATTN_WIDTH = XATTN_HEADS * XATTN_HEAD_DIM

D_FF_DENSE = 2816
N_EXPERTS = 8
TOP_K = 2
D_FF_EXPERT = 3584
N_DENSE = (DEPTH + 1) // 2
N_MOE = DEPTH // 2

EPS = 1e-6

kernel_name = "hybrid_dilated_pool_conv_moe_trunk"

def rmsnorm(x, g):
    xf = x.astype(jnp.float32)
    xf = xf * lax.rsqrt(jnp.mean(xf * xf, axis=-1, keepdims=True) + EPS)
    return xf.astype(x.dtype) * g

def _t5_causal_bucket(dist):
    max_exact = REL_BUCKETS // 2
    d = np.maximum(dist, 1).astype(np.float32)
    large = max_exact + (np.log(d / max_exact) / np.log(REL_MAX_DIST / max_exact)
                         * (REL_BUCKETS - max_exact)).astype(np.int32)
    large = np.minimum(large, REL_BUCKETS - 1)
    return np.where(dist < max_exact, dist, large).astype(np.int32)

def dilated_attention(q, k, v, rel_bias):
    B, S, H, Dh = q.shape
    scale = Dh ** -0.5
    span = Q_BLOCK + MAX_WINDOW
    k_pad = jnp.pad(k, ((0, 0), (MAX_WINDOW, 0), (0, 0), (0, 0)))
    v_pad = jnp.pad(v, ((0, 0), (MAX_WINDOW, 0), (0, 0), (0, 0)))
    q_loc = np.arange(Q_BLOCK)
    branches = []
    for window, dil in DILATED_BRANCHES:
        offs = dil * np.arange(window // dil + 1)
        idx = q_loc[:, None] + MAX_WINDOW - offs[None, :]
        rel_pos = q_loc[:, None] - offs[None, :]
        bias = rel_bias[_t5_causal_bucket(offs)].T.astype(jnp.float32)
        branches.append((idx, rel_pos, bias))

    def block(i):
        t0 = i * Q_BLOCK
        qb = lax.dynamic_slice_in_dim(q, t0, Q_BLOCK, axis=1)
        kb = lax.dynamic_slice_in_dim(k_pad, t0, span, axis=1)
        vb = lax.dynamic_slice_in_dim(v_pad, t0, span, axis=1)
        outs, lses = [], []
        for idx, rel_pos, bias in branches:
            kg = kb[:, idx]
            vg = vb[:, idx]
            logits = jnp.einsum('bqhd,bqjhd->bhqj', qb, kg).astype(jnp.float32) * scale
            logits = logits + bias[None, :, None, :]
            valid = (t0 + rel_pos) >= 0
            logits = jnp.where(valid[None, None], logits, NEG_INF)
            lse = jax.nn.logsumexp(logits, axis=-1)
            p = jnp.exp(logits - lse[..., None]).astype(vg.dtype)
            outs.append(jnp.einsum('bhqj,bqjhd->bqhd', p, vg))
            lses.append(lse)
        w = jax.nn.softmax(jnp.stack(lses, axis=0), axis=0)
        w = jnp.transpose(w, (0, 1, 3, 2))[..., None].astype(q.dtype)
        return jnp.sum(w * jnp.stack(outs, axis=0), axis=0)

    out = lax.map(block, jnp.arange(S // Q_BLOCK))
    return jnp.transpose(out, (1, 0, 2, 3, 4)).reshape(B, S, H * Dh)

def multiscale_pool(u, pool_w, pool_scale):
    B, S, _ = u.shape
    uf = u.astype(jnp.float32).reshape(B, S, POOL_GROUPS, POOL_GROUP_DIM)
    csum = jnp.cumsum(uf, axis=1)
    count_base = jnp.arange(1, S + 1, dtype=jnp.float32)
    outs = []
    for g, w in enumerate(POOL_WINDOWS):
        c = csum[:, :, g]
        lag = jnp.pad(c, ((0, 0), (w, 0), (0, 0)))[:, :S]
        mean = (c - lag) / jnp.minimum(count_base, float(w))[None, :, None]
        outs.append(mean - uf[:, :, g])
    pooled = jnp.stack(outs, axis=2).astype(u.dtype)
    mixed = jnp.einsum('bsgc,gcd->bsgd', pooled, pool_w).reshape(B, S, POOL_WIDTH)
    return mixed * pool_scale

def gated_short_conv(b_gate, c_gate, h, conv_w):
    u = c_gate * h
    y = conv_w[0] * u
    for tap in range(1, CONV_K):
        y = y + conv_w[tap] * jnp.pad(u, ((0, 0), (tap, 0), (0, 0)))[:, :-tap]
    return b_gate * y

def hybrid_mixer(xn, w_in, conv_w, pool_w, pool_scale, w_out, rel_bias):
    B, S, _ = xn.shape
    proj = xn @ w_in
    split_pts = np.cumsum(IN_SPLIT_WIDTHS)[:-1].tolist()
    q, k, v, u_pool, b_gate, c_gate, h_conv = jnp.split(proj, split_pts, axis=-1)
    heads = lambda t: t.reshape(B, S, ATTN_HEADS, ATTN_HEAD_DIM)
    y_attn = dilated_attention(heads(q), heads(k), heads(v), rel_bias)
    y_pool = multiscale_pool(u_pool, pool_w, pool_scale)
    y_conv = gated_short_conv(b_gate, c_gate, h_conv, conv_w)
    y = jnp.concatenate([y_attn, y_pool, y_conv], axis=-1)
    return y @ w_out

def memory_cross_attention(xn, mem_n, wq, wkv, wo):
    B, S, _ = xn.shape
    M = mem_n.shape[1]
    q = (xn @ wq).reshape(B, S, XATTN_HEADS, XATTN_HEAD_DIM)
    k, v = jnp.split(mem_n @ wkv, 2, axis=-1)
    k = k.reshape(B, M, XATTN_HEADS, XATTN_HEAD_DIM)
    v = v.reshape(B, M, XATTN_HEADS, XATTN_HEAD_DIM)
    logits = jnp.einsum('bshd,bmhd->bhsm', q, k).astype(jnp.float32) * (XATTN_HEAD_DIM ** -0.5)
    p = jax.nn.softmax(logits, axis=-1).astype(v.dtype)
    o = jnp.einsum('bhsm,bmhd->bshd', p, v).reshape(B, S, XATTN_WIDTH)
    return o @ wo

def swiglu(x, w13, w2):
    g, u = jnp.split(x @ w13, 2, axis=-1)
    return (jax.nn.silu(g) * u) @ w2

def moe_swiglu(xn, router_w, w13, w2):
    B, S, D = xn.shape
    xt = xn.reshape(B * S, D)
    logits = (xt @ router_w).astype(jnp.float32)
    top_vals, top_idx = lax.top_k(logits, TOP_K)
    top_p = jax.nn.softmax(top_vals, axis=-1)
    gates = jnp.sum(jax.nn.one_hot(top_idx, N_EXPERTS, dtype=jnp.float32) * top_p[..., None],
                    axis=1).astype(xn.dtype)
    out = jnp.zeros_like(xt)
    for e in range(N_EXPERTS):
        out = out + gates[:, e:e + 1] * swiglu(xt, w13[e], w2[e])
    return out.reshape(B, S, D)

def setup_inputs(seed: int = 0) -> dict:
    key = jax.random.key(seed)
    ks = jax.random.split(key, 24)
    f32 = jnp.float32

    def w(k, shape, fan_in):
        return jax.random.normal(k, shape, f32) * (fan_in ** -0.5)

    def gain(k, shape):
        return 1.0 + 0.02 * jax.random.normal(k, shape, f32)

    return {
        "x": jax.random.normal(ks[0], (BATCH, SEQ, D_MODEL), f32),
        "mem": jax.random.normal(ks[1], (BATCH, MEM_LEN, D_MODEL), f32),
        "rel_bias": 0.5 * jax.random.normal(ks[2], (REL_BUCKETS, ATTN_HEADS), f32),
        "mem_norm_g": gain(ks[3], (D_MODEL,)),
        "mix_norm_g": gain(ks[4], (DEPTH, D_MODEL)),
        "w_in": w(ks[5], (DEPTH, D_MODEL, IN_PROJ_WIDTH), D_MODEL),
        "conv_w": w(ks[6], (DEPTH, CONV_K, CONV_WIDTH), CONV_K),
        "pool_w": w(ks[7], (DEPTH, POOL_GROUPS, POOL_GROUP_DIM, POOL_GROUP_DIM), POOL_GROUP_DIM),
        "pool_scale": gain(ks[8], (DEPTH, POOL_WIDTH)) + 0.1 * jax.random.normal(ks[9], (DEPTH, POOL_WIDTH), f32),
        "w_out": w(ks[10], (DEPTH, MIX_WIDTH, D_MODEL), MIX_WIDTH),
        "xattn_norm_g": gain(ks[11], (DEPTH, D_MODEL)),
        "wq_x": w(ks[12], (DEPTH, D_MODEL, XATTN_WIDTH), D_MODEL),
        "wkv_x": w(ks[13], (DEPTH, D_MODEL, 2 * XATTN_WIDTH), D_MODEL),
        "wo_x": w(ks[14], (DEPTH, XATTN_WIDTH, D_MODEL), XATTN_WIDTH),
        "ffn_norm_g": gain(ks[15], (DEPTH, D_MODEL)),
        "w13_dense": w(ks[16], (N_DENSE, D_MODEL, 2 * D_FF_DENSE), D_MODEL),
        "w2_dense": w(ks[17], (N_DENSE, D_FF_DENSE, D_MODEL), D_FF_DENSE),
        "router_w": w(ks[18], (N_MOE, D_MODEL, N_EXPERTS), D_MODEL),
        "w13_moe": w(ks[19], (N_MOE, N_EXPERTS, D_MODEL, 2 * D_FF_EXPERT), D_MODEL),
        "w2_moe": w(ks[20], (N_MOE, N_EXPERTS, D_FF_EXPERT, D_MODEL), D_FF_EXPERT),
        "final_norm_g": gain(ks[21], (D_MODEL,)),
    }

def reference(x, mem, rel_bias, mem_norm_g, mix_norm_g, w_in, conv_w, pool_w, pool_scale,
              w_out, xattn_norm_g, wq_x, wkv_x, wo_x, ffn_norm_g, w13_dense, w2_dense,
              router_w, w13_moe, w2_moe, final_norm_g):
    mem_n = rmsnorm(mem, mem_norm_g)
    for layer in range(DEPTH):
        x = x + hybrid_mixer(rmsnorm(x, mix_norm_g[layer]), w_in[layer], conv_w[layer],
                             pool_w[layer], pool_scale[layer], w_out[layer], rel_bias)
        x = x + memory_cross_attention(rmsnorm(x, xattn_norm_g[layer]), mem_n,
                                       wq_x[layer], wkv_x[layer], wo_x[layer])
        hn = rmsnorm(x, ffn_norm_g[layer])
        if layer % 2 == 0:
            x = x + swiglu(hn, w13_dense[layer // 2], w2_dense[layer // 2])
        else:
            x = x + moe_swiglu(hn, router_w[layer // 2], w13_moe[layer // 2], w2_moe[layer // 2])
    return rmsnorm(x, final_norm_g)


_drawn_inputs = setup_inputs


def setup_inputs(seed=0):
    import zlib

    import numpy as np

    out = dict(_drawn_inputs(seed))
    spreads = {}
    factors = {'mem_norm_g': 4.799, 'xattn_norm_g': 8.0, 'final_norm_g': 7.555, 'ffn_norm_g': 3.043}
    for name, (base, spread) in spreads.items():
        noise = np.random.default_rng([zlib.crc32(name.encode()), seed]).standard_normal(out[name].shape)
        drawn = base * np.exp(spread * noise) if base else spread * noise
        out[name] = __import__('jax').numpy.asarray(drawn.astype(out[name].dtype))
    for name, factor in factors.items():
        out[name] = (out[name] * factor).astype(out[name].dtype)
    return out
```

```python
from contextlib import ExitStack

import numpy as np

import concourse.bass as bass
from concourse import mybir

F32, F32R, I32, BF16 = mybir.dt.float32, mybir.dt.float32r, mybir.dt.int32, mybir.dt.bfloat16
ACT = mybir.ActivationFunctionType
ALU = mybir.AluOpType
AX = mybir.AxisListType

P = 128
D = 1024
KD = D // P
T = 256
NT = T // P
DEPTH = 2
EPS = 1e-6

HEADS, DH = 8, 64
PAIRS = HEADS // 2
WINDOWS = ((128, 1), (512, 4), (2048, 16))
BUCKETS, MAX_DIST = 32, 128
MASKED = -1e30

XHEADS, XDH = 4, 128
XW = XHEADS * XDH
XSCALE = XDH ** -0.5
IN_W = 2560

FD = 2816
FE = 3584
NE = 8
OVER = 3
ITEMS = NE + OVER

FT = 512
UNIT = 2048
RAW = 6
SPLIT = 3

LAYER_UNITS = 24
DENSE_UNITS = 36
ITEM_UNITS = 6 * (FE // FT)
DENSE_STEPS = FD // FT
ITEM_STEPS = FE // FT
MOE_BASE = DEPTH * LAYER_UNITS + DENSE_UNITS

DVE_LAYER = 52

SKEW_W = 384


def _bucket(dist):
    exact = BUCKETS // 2
    d = np.maximum(dist, 1).astype(np.float32)
    large = exact + (np.log(d / exact) / np.log(MAX_DIST / exact) * (BUCKETS - exact)).astype(np.int32)
    large = np.minimum(large, BUCKETS - 1)
    return np.where(dist < exact, dist, large).astype(np.int32)


def shape_constants():
    table = np.zeros((BUCKETS + 1, SKEW_W), np.float32)
    for i in range(SKEW_W):
        dist = T - 1 - i
        reach = sum(1 for w, d in WINDOWS if 0 <= dist <= w and dist % d == 0) if dist >= 0 else 0
        if reach:
            table[int(_bucket(np.array(dist))), i] = 1.0
            table[BUCKETS, i] = np.log(float(reach))
        else:
            table[BUCKETS, i] = MASKED
    inv = np.zeros((P, 2, T), np.float32)
    for g, w in enumerate((2, 4, 8, 16)):
        inv[(g % 2) * 64:(g % 2) * 64 + 64, g // 2, :] = 1.0 / np.minimum(np.arange(1, T + 1), w)
    mats = np.zeros((P, 4, P), np.float32)
    mats[:, 0, :] = np.eye(P)
    mats[:, 1, :] = np.triu(np.ones((P, P)), 1)
    mats[:, 2, :] = 1.0
    mats[:, 3, :] = np.arange(P)[None, :]
    less8 = np.tile(np.arange(NE, dtype=np.float32) - NE, (P, NT, 1))
    return {"bias_table": table, "pool_inv": inv, "mats": mats, "less8": less8}


class Chain:

    def __init__(self, eng, sem):
        self.eng, self.sem, self.base, self.n = eng, sem, 0, 0

    def step(self, ins):
        ins.then_inc(self.sem, 1)
        self.n += 1
        return ins

    def wait(self):
        self.eng.wait_ge(self.sem, self.base + self.n)

    def link(self, ins):
        self.step(ins)
        self.wait()

    def restart(self, base):
        self.base, self.n = base, 0


class Stream:

    def __init__(self, first, rounds):
        self.halves, self.rounds = first * 2, rounds

    def upto(self, u, half=1):
        return self.halves + (2 * u + half + 1)

    def landed(self, u):
        return (self.rounds + (u // RAW + 1)) * 16


def build(nc, io):
    with ExitStack() as ctx:
        _build(nc, io, ctx)


def _build(nc, io, ctx):
    def sb(name, shape, dt=F32):
        return ctx.enter_context(nc.sbuf_tensor(name, shape, dt))

    sems = {}

    def sem(name):
        if name not in sems:
            sems[name] = ctx.enter_context(nc.semaphore(name))
        return sems[name]

    raw = sb("raw", [P, RAW, UNIT])
    w_hi = sb("w_hi", [P, SPLIT, 2, UNIT // 2], F32R)
    w_lo = sb("w_lo", [P, SPLIT, 2, UNIT // 2], F32R)
    x = sb("x", [P, NT, D])
    xn = sb("xn", [P, NT, D])
    xT_hi = sb("xT_hi", [P, KD, T], F32R)
    xT_lo = sb("xT_lo", [P, KD, T], F32R)
    memT_hi = sb("memT_hi", [P, KD, T], F32R)
    memT_lo = sb("memT_lo", [P, KD, T], F32R)
    yT_hi = sb("yT_hi", [P, KD, T], F32R)
    yT_lo = sb("yT_lo", [P, KD, T], F32R)
    g_row = sb("g_row", [P, D])
    bias = sb("bias", [P, HEADS, T])
    qk = sb("qk", [P, 2, PAIRS, T])
    v = sb("v", [P, NT, 512])
    prob = sb("prob", [P, 2, 512])
    probT = sb("probT", [P, 2, 512])
    conv_u = sb("conv_u", [P, 2, T + 2])
    pool_a = sb("pool_a", [P, 2, T + 16])
    pool_b = sb("pool_b", [P, 2, T + 16])
    pool_inv = sb("pool_inv", [P, 2, T])
    mats = sb("mats", [P, 4, P])
    zeros = sb("zeros", [P, 512], BF16)
    conv_w = sb("conv_w", [P, 3, 2])
    pool_w = sb("pool_w", [P, 2, 64])
    pool_s = sb("pool_s", [P, 2])
    rel = sb("rel", [BUCKETS + 1, HEADS])
    table = sb("table", [BUCKETS + 1, SKEW_W])
    eps_col = sb("eps_col", [P, 1])
    ss = sb("ss", [P, NT])
    lnv = sb("lnv", [P, NT])
    r0 = sb("r0", [P, NT])
    nw = sb("nw", [P, 3, NT])
    rstd = sb("rstd", [P, NT])
    mx = sb("mx", [P, 2, NT])
    nmx = sb("nmx", [P, 2, NT])
    den = sb("den", [P, NT, HEADS])
    rden = sb("rden", [P, NT, HEADS])
    router = sb("router", [P, KD, NE])
    router_hi = sb("router_hi", [P, KD, NE], F32R)
    router_lo = sb("router_lo", [P, KD, NE], F32R)
    less8 = sb("less8", [P, NT, NE])
    lg = sb("lg", [P, NT, NE])
    tmp8 = sb("tmp8", [P, NT, NE])
    sel1 = sb("sel1", [P, NT, NE])
    sel2 = sb("sel2", [P, NT, NE])
    mask = sb("mask", [P, NT, NE])
    gates = sb("gates", [P, NT, NE])
    top = sb("top", [P, 8, NT])
    over = sb("over", [P, NE])
    pick = sb("pick", [P, OVER, NE])
    first = sb("first", [P, OVER + 1])
    places = sb("places", [P, ITEMS + 1, 2, NT])
    now = sb("now", [P, 2, 2, NT])
    info = sb("info", [1, OVER + 1], I32)
    S = prob[:, 0, 0:NT * P].rearrange("p (t r) -> p t r", t=NT)
    Sg = prob[:, 1, 0:NT * P].rearrange("p (t r) -> p t r", t=NT)
    SgT = probT[:, 0, 0:NT * P].rearrange("p (t r) -> p t r", t=NT)

    bank = [ctx.enter_context(nc.psum_tensor(f"bank{i}", [P, 512], F32)) for i in range(8)]
    skew = nc.dram_tensor("skew", [HEADS, P, SKEW_W], F32, kind="Internal")

    ident = mats[:, 0, :]
    before = mats[:, 1, :]
    ones = mats[:, 2, :]
    iota = mats[:, 3, :]
    xn_flat = xn[:, :, :].rearrange("p t d -> p (t d)")
    qk_flat = qk[:, :, :, :].rearrange("p a b t -> p (a b t)")
    mem_sb = qk_flat.rearrange("p (t d) -> p t d", t=NT)
    conv_c = xn_flat[:, 0:512].rearrange("p (b t) -> p b t", b=2)
    conv_y = xn_flat[:, 512:1024].rearrange("p (b t) -> p b t", b=2)
    pooled = xn_flat[:, 1024:1536].rearrange("p (b t) -> p b t", b=2)
    y_tok = xn_flat[:, 0:1024].rearrange("p (t f) -> p t f", t=NT)
    hid = qk_flat[:, 0:1024].rearrange("p (t f) -> p t f", t=NT)
    y_sb = qk_flat[:, 1024:2048]
    xgT_hi = yT_hi[:, 4:8, :].rearrange("p k t -> p (k t)").rearrange("p (k r) -> p k r", k=KD)
    xgT_lo = yT_lo[:, 4:8, :].rearrange("p k t -> p (k t)").rearrange("p (k r) -> p k r", k=KD)
    bias_flat = bias[:, :, :].rearrange("p h c -> p (h c)")

    def skew_stage(h):
        if h < 5:
            return bias_flat[:, h * SKEW_W:(h + 1) * SKEW_W]
        return (prob[:, h - 5, 0:SKEW_W] if h < 7 else probT[:, 0, 0:SKEW_W])

    def banks4(b):
        return bank[b][:, :].rearrange("p (k t) -> p k t", t=P)

    SCATTER = (3, 1, 6, 7)
    block = ctx.enter_context(nc.Block())

    def used(eng, st, u):
        eng.wait_ge(sem("unit_used"), st.upto(u) + 2 * SPLIT)

    def hold(eng, name, count):
        eng.wait_ge(sem(name), count)
        eng.sem_inc(sem("held"), 1)

    @block.sync
    def _(sp):
        def load(st, u, src, width=UNIT):
            hold(sp, "raw_free", st.upto(u))
            dst = raw[:, u % RAW, 0:width]
            n = src.shape[-1]
            sp.dma_start(dst.rearrange("p (k c) -> p k c", c=n), src).then_inc(sem(f"raw{u % RAW}"), 16)

        def rows(w, k0, kn, c0, cn):
            return w.rearrange("(k p) c -> p k c", p=P)[:, k0:k0 + kn, c0:c0 + cn] if isinstance(c0, int) \
                else w.rearrange("(k p) c -> p k c", p=P)[:, k0:k0 + kn, bass.ds(c0, cn)]

        def up_units(st, u, w, width, col):
            for m in range(2):
                load(st, u + m, rows(w, 4 * m, 4, col, width), 4 * width)

        def down_units(st, u, w, j, half=False):
            n = 1 if half else 2
            for m in range(2):
                f0 = j * FT + m * n * P
                src = w[f0:f0 + n * P] if isinstance(f0, int) else w[bass.ds(f0, n * P)]
                load(st, u + m, src.rearrange("(k p) c -> p k c", p=P), n * D)

        sp.dma_start(mem_sb, io["mem"][0].rearrange("(t p) d -> p t d", p=P)).then_inc(sem("mem_in"), 16)
        sp.dma_start(x[:, :, :], io["x"][0].rearrange("(t p) d -> p t d", p=P)).then_inc(sem("x_in"), 16)

        with sp.Fori(0, DEPTH) as l:
            st = Stream(l * (LAYER_UNITS + DENSE_UNITS), l * ((LAYER_UNITS + DENSE_UNITS) // RAW))
            w_in, w_out = io["w_in"][l], io["w_out"][l]
            for c in range(IN_W // 512):
                up_units(st, 2 * c, w_in, 512, c * 512)
            for i, (c, k) in enumerate(((0, 4), (1, 4), (0, 0), (1, 0))):
                load(st, 10 + i, rows(w_out, k, 4, c * 512, 512))
            up_units(st, 14, io["wkv_x"][l], 512, 0)
            up_units(st, 16, io["wkv_x"][l], 512, 512)
            up_units(st, 18, io["wq_x"][l], 512, 0)
            for i in range(4):
                load(st, 20 + i, rows(io["wo_x"][l], 2 * (i % 2), 2, (i // 2) * 512, 512), 1024)
            with sp.If(l < 1):
                st = Stream(LAYER_UNITS, LAYER_UNITS // RAW)
                w13, w2 = io["w13_dense"][0], io["w2_dense"][0]
                up_units(st, 0, w13, FT, FD)
                up_units(st, 2, w13, FT, 0)
                with sp.Fori(1, DENSE_STEPS) as j:
                    sj = Stream(LAYER_UNITS + (j - 1) * 6, LAYER_UNITS // RAW + (j - 1))
                    up_units(sj, 4, w13, FT, FD + j * FT)
                    up_units(sj, 6, w13, FT, j * FT)
                    down_units(sj, 8, w2, j - 1)
                e = 4 + 6 * (DENSE_STEPS - 1)
                up_units(st, e, w13, FT // 2, FD + DENSE_STEPS * FT)
                up_units(st, e + 2, w13, FT // 2, DENSE_STEPS * FT)
                down_units(st, e + 4, w2, DENSE_STEPS - 1)
                down_units(st, e + 6, w2, DENSE_STEPS, half=True)

        def item(i, w13, w2):
            st = Stream(i * ITEM_UNITS + MOE_BASE, i * (ITEM_UNITS // RAW) + MOE_BASE // RAW)
            up_units(st, 0, w13, FT, FE)
            up_units(st, 2, w13, FT, 0)
            with sp.Fori(1, ITEM_STEPS) as j:
                sj = Stream(i * ITEM_UNITS + (j - 1) * 6 + MOE_BASE,
                            i * (ITEM_UNITS // RAW) + (j - 1) + MOE_BASE // RAW)
                up_units(sj, 4, w13, FT, j * FT + FE)
                up_units(sj, 6, w13, FT, j * FT)
                down_units(sj, 8, w2, j - 1)
            down_units(st, 4 + 6 * (ITEM_STEPS - 1), w2, ITEM_STEPS - 1)

        with sp.Fori(0, NE) as i:
            item(i, io["w13_moe"][0, i], io["w2_moe"][0, i])
        sp.wait_ge(sem("info_ready"), 1)
        n_items = sp.value_load(info[0:1, 0:1], min_val=NE, max_val=ITEMS)
        with sp.Fori(NE, ITEMS) as i:
            with sp.If(n_items > i):
                e = sp.value_load(info[0:1, bass.ds(i - (NE - 1), 1)], min_val=0, max_val=NE - 1)
                item(i, io["w13_moe"][0, e], io["w2_moe"][0, e])
            sp.nop()
        for t in range(NT):
            sp.wait_ge(sem("xn_ready"), 2 * (3 * DEPTH + 1) + t + 1)
            sp.dma_start(io["out"][0, t * P:(t + 1) * P, :], xn[:, t, :]).then_inc(sem("out_done"), 16)
        sp.wait_ge(sem("out_done"), 16 * NT)

    @block.gpsimd
    def _(pool):
        pool.dma_start(mats[:, :, :], io["mats"]).then_inc(sem("mats_in"), 16)

        def load_gain(m, src):
            if not (isinstance(m, int) and m == 0):
                hold(pool, "xn_ready", m * 2)
            pool.dma_start(g_row[:, :], src).then_inc(sem("gain_in"), 16)

        def gain(ap, l=None):
            row = ap.rearrange("(o d) -> o d", o=1) if l is None else ap[l].rearrange("(o d) -> o d", o=1)
            return row.broadcast_to([P, D])

        load_gain(0, gain(io["mem_norm_g"]))
        pool.memset(rel[:, :], 1.0).then_inc(sem("rel_ones"), 1)
        pool.wait_ge(sem("rel_ones"), 1)
        pool.dma_start(rel[0:BUCKETS, :], io["rel_bias"]).then_inc(sem("table_in"), 16)
        pool.dma_start(table[:, :], io["bias_table"]).then_inc(sem("table_in"), 16)
        pool.dma_start(pool_inv[:, :, :], io["pool_inv"]).then_inc(sem("params_in"), 16)
        pool.dma_start(router[:, :, :], io["router_w"][0].rearrange("(k p) e -> p k e", p=P))\
            .then_inc(sem("router_in"), 16)
        pool.dma_start(less8[:, :, :], io["less8"]).then_inc(sem("router_in"), 16)
        pool.wait_ge(sem("skew_rows"), HEADS)
        for h in range(HEADS):
            pool.dma_start(skew.ap()[h], skew_stage(h)).then_inc(sem("skew_out"), 16)
        pool.wait_ge(sem("skew_out"), 16 * HEADS)
        for h in range(HEADS):
            pool.dma_start(bias[:, h, :], bass.AP(skew, h * P * SKEW_W + P - 1, [[SKEW_W - 1, P], [1, T]]))\
                .then_inc(sem("bias_in"), 16)
        with pool.Fori(0, DEPTH) as l:
            load_gain(l * 3 + 1, gain(io["mix_norm_g"], l))
            hold(pool, "x_ready", l * 3 + 1)
            pool.dma_start(conv_w[:, :, :], io["conv_w"][l].rearrange("k (b p) -> p k b", p=P), allow_slow_non_contiguous=True)\
                .then_inc(sem("params_in"), 16)
            pool.dma_start(pool_w[:, :, :], io["pool_w"][l].rearrange("(b h) c d -> (h c) b d", h=2))\
                .then_inc(sem("params_in"), 16)
            pool.dma_start(pool_s[:, :], io["pool_scale"][l].rearrange("(b p) -> p b", p=P), allow_slow_non_contiguous=True)\
                .then_inc(sem("params_in"), 16)
            load_gain(l * 3 + 2, gain(io["xattn_norm_g"], l))
            load_gain(l * 3 + 3, gain(io["ffn_norm_g"], l))
        load_gain(3 * DEPTH + 1, gain(io["final_norm_g"]))

    @block.scalar
    def _(act):
        def hi(st, u, width=UNIT):
            act.wait_ge(sem(f"raw{u % RAW}"), st.landed(u))
            n = width // 2
            for half in range(2):
                act.wait_ge(sem("unit_used"), st.upto(u, half))
                act.activation(w_hi[:, u % SPLIT, half, 0:n], raw[:, u % RAW, half * n:(half + 1) * n], ACT.Copy)\
                    .then_inc(sem("unit_hi"), 1)

        def norm(m, src, banks, dst):
            act.activation(xn[:, 1, :], src[:, 1, :], ACT.Square, accum_out=ss[:, 1:2])\
                .then_inc(sem("square_act"), 1)
            act.wait_ge(sem("square_act"), m + 1)
            act.wait_ge(sem("square_dve"), m + 1)
            act.activation(lnv[:, :], ss[:, :], ACT.Ln, scale=1.0 / D, bias=eps_col[:, 0:1])\
                .then_inc(sem("ln_act"), 1)
            act.wait_ge(sem("ln_act"), m + 1)
            act.activation(r0[:, :], lnv[:, :], ACT.Exp, scale=-0.5).then_inc(sem("rstd_guess"), 1)
            for i in range(4 if banks else 0):
                t, half = i // 2, i % 2
                act.wait_ge(sem("xT_mm"), m * 4 + i + 1)
                act.activation(dst[:, 4 * half:4 * half + 4, t * P:(t + 1) * P], banks4(banks[i]), ACT.Copy)\
                    .then_inc(sem("xT_hi"), 1)

        def silu_tiles(width, tiles, g_bank):
            for t in range(tiles):
                act.activation(hid[:, t, 0:width], bank[g_bank + t][:, 0:width], ACT.Silu)\
                    .then_inc(sem("silu"), 1)

        def hidT_hi(width, tiles, g_bank):
            for t in range(tiles):
                n = width // P
                act.activation(yT_hi[:, 0:n, t * P:(t + 1) * P], banks4(g_bank + t)[:, 0:n, :], ACT.Copy)\
                    .then_inc(sem("hidT_hi"), 1)

        act.wait_ge(sem("consts"), 1)
        for h in range(0, HEADS, 2):
            act.wait_ge(sem("skew_mm"), h + 1)
            act.activation(skew_stage(h), bank[h][:, 0:SKEW_W], ACT.Copy).then_inc(sem("skew_rows"), 1)
        act.preload_act_table_set("natural_log_exp_and_others")
        act.wait_ge(sem("mem_in"), 16)
        norm(0, mem_sb, (0, 1, 2, 3), memT_hi)
        act.wait_ge(sem("x_in"), 16)

        with act.Fori(0, DEPTH) as l:
            l1 = l + 1
            st = Stream(l * (LAYER_UNITS + DENSE_UNITS), l * ((LAYER_UNITS + DENSE_UNITS) // RAW))
            act.preload_act_table_set("natural_log_exp_and_others")
            act.wait_ge(sem("x_ready"), l * 3 + 1)
            norm(l * 3 + 1, x, (0, 1, 2, 3), xT_hi)
            for u in range(4):
                hi(st, u)
            used(act, st, 1)
            for b in range(2):
                act.activation(qk[:, 0, 2 * b:2 * b + 2, :], bank[4 + b][:, :].rearrange("p (c t) -> p c t", c=2),
                               ACT.Copy, scale=DH ** -0.5).then_inc(sem("q_sb"), 1)
            for u in range(4, 8):
                hi(st, u)
            used(act, st, 5)
            for t in range(NT):
                act.activation(v[:, t, :], bank[t][:, :], ACT.Copy).then_inc(sem("v_sb"), 1)
            hi(st, 8)
            hi(st, 9)
            used(act, st, 9)
            act.activation(conv_c, bank[4][:, :].rearrange("p (b t) -> p b t", b=2), ACT.Copy)\
                .then_inc(sem("c_sb"), 1)
            for u in range(10, 13):
                hi(st, u)
            act.wait_ge(sem("pool_mm"), l1)
            act.wait_ge(sem("params_in"), l * 48 + 64)
            for b in range(2):
                act.activation(yT_hi[:, 4 + b, :], bank[2][:, b * T:(b + 1) * T], ACT.Copy, scale=pool_s[:, b:b + 1])\
                    .then_inc(sem("yT_hi"), 1)
            act.wait_ge(sem("conv_y"), l1)
            act.activation(yT_hi[:, 6:8, :], conv_y, ACT.Copy).then_inc(sem("yT_hi"), 1)
            for h in range(HEADS):
                act.wait_ge(sem("logits"), l * HEADS + h + 1)
                for t, (a, b) in enumerate(((0, P), (P, 3 * P))):
                    act.activation(prob[:, h % 2, a:b], prob[:, h % 2, a:b], ACT.Exp, bias=nmx[:, h % 2, t:t + 1],
                                   accum_out=den[:, t, h:h + 1]).then_inc(sem("exp"), 1)
            for t in range(NT):
                act.wait_ge(sem("yTok_mm"), l * 2 + t + 1)
                act.activation(yT_hi[:, 0:4, t * P:(t + 1) * P], banks4(6 + t), ACT.Copy).then_inc(sem("yT_hi"), 1)
            for u in range(13, 17):
                hi(st, u)
            act.preload_act_table_set("natural_log_exp_and_others")
            act.wait_ge(sem("x_ready"), l * 3 + 2)
            norm(l * 3 + 2, x, (0, 1, 2, 3), xT_hi)
            hi(st, 17)
            used(act, st, 15)
            for b in range(2):
                act.activation(qk[:, 1, 2 * b:2 * b + 2, :], bank[4 + b][:, :].rearrange("p (c t) -> p c t", c=2),
                               ACT.Copy).then_inc(sem("xk_sb"), 1)
            hi(st, 18)
            hi(st, 19)
            used(act, st, 17)
            for t in range(NT):
                act.activation(v[:, t, :], bank[6 + t][:, :], ACT.Copy).then_inc(sem("xv_sb"), 1)
            used(act, st, 19)
            for b in range(2):
                act.activation(qk[:, 0, 2 * b:2 * b + 2, :], bank[4 + b][:, :].rearrange("p (c t) -> p c t", c=2),
                               ACT.Copy).then_inc(sem("xq_sb"), 1)
            for h in range(XHEADS):
                act.wait_ge(sem("xmax"), l * XHEADS + h + 1)
                if h >= 2:
                    act.wait_ge(sem("xprobT_mm"), l * XHEADS + h - 1)
                for t in range(NT):
                    act.activation(prob[:, h % 2, t * T:(t + 1) * T], bank[6 + h % 2][:, t * T:(t + 1) * T], ACT.Exp,
                                   scale=XSCALE, bias=nmx[:, h % 2, t:t + 1],
                                   accum_out=den[:, t, h:h + 1]).then_inc(sem("xexp"), 1)
            for t in range(NT):
                act.wait_ge(sem("xyT_mm"), l * 2 + t + 1)
                act.activation(yT_hi[:, 0:4, t * P:(t + 1) * P], banks4(4 + t), ACT.Copy).then_inc(sem("xyT_hi"), 1)
            for u in range(20, 24):
                hi(st, u, 1024)
            act.preload_act_table_set("natural_log_exp_and_others")
            act.wait_ge(sem("x_ready"), l * 3 + 3)
            norm(l * 3 + 3, x, (4, 5, 6, 7), xT_hi)
            with act.If(l < 1):
                st = Stream(LAYER_UNITS, LAYER_UNITS // RAW)
                act.preload_act_table(ACT.Silu)
                for u in range(4):
                    hi(st, u)
                used(act, st, 3)
                silu_tiles(FT, NT, 2)
                with act.Fori(1, DENSE_STEPS) as j:
                    sj = Stream(LAYER_UNITS + (j - 1) * 6, LAYER_UNITS // RAW + (j - 1))
                    hi(sj, 4)
                    hi(sj, 5)
                    act.wait_ge(sem("hidT_mm"), j)
                    hidT_hi(FT, NT, 2)
                    for u in range(6, 10):
                        hi(sj, u)
                    used(act, sj, 7)
                    silu_tiles(FT, NT, 2)
                e = 4 + 6 * (DENSE_STEPS - 1)
                hi(st, e, 1024)
                hi(st, e + 1, 1024)
                act.wait_ge(sem("hidT_mm"), DENSE_STEPS)
                hidT_hi(FT, NT, 2)
                hi(st, e + 2, 1024)
                hi(st, e + 3, 1024)
                hi(st, e + 4)
                hi(st, e + 5)
                used(act, st, e + 3)
                silu_tiles(FT // 2, NT, 2)
                hi(st, e + 6, 1024)
                act.wait_ge(sem("hidT_mm"), DENSE_STEPS + 1)
                hidT_hi(FT // 2, NT, 2)
                hi(st, e + 7, 1024)
            act.nop()

        act.wait_ge(sem("router_in"), 32)
        act.activation(router_hi[:, :, :], router[:, :, :], ACT.Copy).then_inc(sem("router_hi"), 1)
        act.wait_ge(sem("top_diff"), 1)
        act.activation(top[:, 2, :], top[:, 1, :], ACT.Exp).then_inc(sem("top_exp"), 1)
        act.wait_ge(sem("info_ready"), 1)
        n_items = act.value_load(info[0:1, 0:1], min_val=NE, max_val=ITEMS)
        act.preload_act_table(ACT.Silu)

        def gathered_hi(i):
            for b in range(2):
                act.wait_ge(sem("gather_mm"), i * 2 + b + 1)
                act.activation(xgT_hi[:, 4 * b:4 * b + 4, :], banks4(6 + b), ACT.Copy).then_inc(sem("gather_hi"), 1)

        def rows_out(i):
            act.wait_ge(sem("unit_used"), i * (2 * ITEM_UNITS) + 2 * (MOE_BASE + SPLIT))
            for col in range(2):
                act.activation(y_sb[:, col * 512:(col + 1) * 512], bank[4 + col][:, :], ACT.Copy)\
                    .then_inc(sem("rows_sb"), 1)

        act.sem_inc(sem("rows_sb"), 2)
        gathered_hi(0)
        MO = DENSE_STEPS + 1
        MT = NT * MO
        with act.Fori(0, ITEMS) as i:
            with act.If(n_items > i):
                st = Stream(i * ITEM_UNITS + MOE_BASE, i * (ITEM_UNITS // RAW) + MOE_BASE // RAW)
                hi(st, 0)
                hi(st, 1)
                with act.If(i > 0):
                    rows_out(i)
                hi(st, 2)
                hi(st, 3)
                used(act, st, 3)
                silu_tiles(FT, 1, 2)
                with act.Fori(1, ITEM_STEPS) as j:
                    sj = Stream(i * ITEM_UNITS + (j - 1) * 6 + MOE_BASE,
                                i * (ITEM_UNITS // RAW) + (j - 1) + MOE_BASE // RAW)
                    hi(sj, 4)
                    hi(sj, 5)
                    act.wait_ge(sem("hidT_mm"), i * ITEM_STEPS + j + MO)
                    hidT_hi(FT, 1, 2)
                    for u in range(6, 10):
                        hi(sj, u)
                    used(act, sj, 7)
                    silu_tiles(FT, 1, 2)
                e = 4 + 6 * (ITEM_STEPS - 1)
                hi(st, e)
                hi(st, e + 1)
                act.wait_ge(sem("hidT_mm"), i * ITEM_STEPS + ITEM_STEPS + MO)
                hidT_hi(FT, 1, 2)
                gathered_hi(i + 1)
            act.nop()
        rows_out(n_items)
        act.preload_act_table_set("natural_log_exp_and_others")
        act.wait_ge(sem("x_final"), 1)
        norm(3 * DEPTH + 1, x, None, None)

    @block.vector
    def _(dve):
        c = Chain(dve, sem("dve_step"))

        def lo(st, u, width=UNIT):
            n = width // 2
            for half in range(2):
                dve.wait_ge(sem("unit_hi"), st.upto(u, half))
                dve.tensor_tensor(w_lo[:, u % SPLIT, half, 0:n], raw[:, u % RAW, half * n:(half + 1) * n],
                                  w_hi[:, u % SPLIT, half, 0:n].bitcast(F32), ALU.subtract)\
                    .then_inc(sem("raw_free"), 1)

        def rest(out, src, hi_part):
            return dve.tensor_tensor(out, src, hi_part.bitcast(F32), ALU.subtract)

        def norm(m, src, banks, dst_hi, dst_lo):
            dve.tensor_tensor_reduce(xn[:, 0, :], src[:, 0, :], src[:, 0, :], 1.0, 0.0, ALU.mult, ALU.add,
                                     ss[:, 0:1]).then_inc(sem("square_dve"), 1)
            dve.wait_ge(sem("square_dve"), m + 1)
            dve.wait_ge(sem("rstd_guess"), m + 1)
            c.step(dve.tensor_scalar(nw[:, 0, :], ss[:, :], 1.0 / D, EPS, ALU.mult, ALU.add))
            c.link(dve.tensor_tensor(nw[:, 1, :], r0[:, :], r0[:, :], ALU.mult))
            c.link(dve.tensor_tensor(nw[:, 2, :], nw[:, 0, :], nw[:, 1, :], ALU.mult))
            c.link(dve.tensor_scalar(nw[:, 1, :], nw[:, 2, :], -0.5, 1.5, ALU.mult, ALU.add))
            c.link(dve.tensor_tensor(rstd[:, :], r0[:, :], nw[:, 1, :], ALU.mult))
            dve.wait_ge(sem("gain_in"), m * 16 + 16)
            for t in range(NT):
                dve.scalar_tensor_tensor(xn[:, t, :], src[:, t, :], rstd[:, t:t + 1], g_row[:, :],
                                         ALU.mult, ALU.mult).then_inc(sem("xn_ready"), 1)
            for i in range(4 if banks else 0):
                t, half = i // 2, i % 2
                dve.wait_ge(sem("xT_hi"), m * 4 + i + 1)
                s = (slice(None), slice(4 * half, 4 * half + 4), slice(t * P, (t + 1) * P))
                rest(dst_lo[s], banks4(banks[i]), dst_hi[s]).then_inc(sem("xT_lo"), 1)

        def add_to_x(st, units, first_bank):
            for col in range(2):
                used(dve, st, units[col])
                for t in range(NT):
                    s = slice(col * 512, (col + 1) * 512)
                    last = dve.tensor_tensor(x[:, t, s], x[:, t, s], bank[first_bank + 2 * col + t][:, :], ALU.add)
            last.then_inc(sem("x_ready"), 1)

        def gate_tiles(width, tiles, silus):
            for t in range(tiles):
                dve.wait_ge(sem("silu"), silus + (t + 1))
                dve.tensor_tensor(hid[:, t, 0:width], hid[:, t, 0:width], bank[t][:, 0:width], ALU.mult)\
                    .then_inc(sem("hid_ready"), 1)

        def hidT_lo(width, tiles, g_bank, his):
            n = width // P
            for t in range(tiles):
                dve.wait_ge(sem("hidT_hi"), his + (t + 1))
                s = (slice(None), slice(0, n), slice(t * P, (t + 1) * P))
                rest(yT_lo[s], banks4(g_bank + t)[:, 0:n, :], yT_hi[s]).then_inc(sem("hidT_lo"), 1)

        dve.sem_inc(sem("raw_free"), 2 * RAW)
        dve.memset(eps_col[:, :], EPS).then_inc(sem("consts"), 1)
        dve.memset(zeros[:, :], 0.0).then_inc(sem("zeros"), 1)
        c.step(dve.memset(conv_u[:, :, :], 0.0))
        c.step(dve.memset(pool_a[:, :, :], 0.0))
        c.step(dve.memset(pool_b[:, :, :], 0.0))
        c.link(dve.memset(places[:, :, :, :], -1.0))
        for h in range(1, HEADS, 2):
            dve.wait_ge(sem("skew_mm"), h + 1)
            dve.tensor_copy(skew_stage(h), bank[h][:, 0:SKEW_W]).then_inc(sem("skew_rows"), 1)
        dve.wait_ge(sem("mem_in"), 16)
        norm(0, mem_sb, (0, 1, 2, 3), memT_hi, memT_lo)
        dve.wait_ge(sem("x_in"), 16)
        dve.sem_inc(sem("x_ready"), 1)
        head = c.n

        with dve.Fori(0, DEPTH) as l:
            l1 = l + 1
            c.restart(l * DVE_LAYER + head)
            st = Stream(l * (LAYER_UNITS + DENSE_UNITS), l * ((LAYER_UNITS + DENSE_UNITS) // RAW))
            dve.wait_ge(sem("x_ready"), l * 3 + 1)
            norm(l * 3 + 1, x, (0, 1, 2, 3), xT_hi, xT_lo)
            for u in range(5):
                lo(st, u)
            used(dve, st, 3)
            for b in range(2):
                dve.tensor_copy(qk[:, 1, 2 * b:2 * b + 2, :], bank[6 + b][:, :].rearrange("p (c t) -> p c t", c=2))\
                    .then_inc(sem("k_sb"), 1)
            for u in range(5, 10):
                lo(st, u)
            used(dve, st, 7)
            A, B = pool_a[:, :, 16:], pool_b[:, :, 16:]
            u_pool = bank[2][:, :].rearrange("p (b t) -> p b t", b=2)

            def back(buf, k):
                return buf[:, :, 16 - k:16 - k + T]

            c.link(dve.tensor_copy(A, u_pool))
            c.link(dve.tensor_tensor(B, A, back(pool_a, 1), ALU.add))
            c.step(dve.tensor_tensor(A[64:128, 0, :], B[64:128, 0, :], back(pool_b, 2)[64:128, 0, :], ALU.add))
            c.link(dve.tensor_tensor(A[:, 1, :], B[:, 1, :], back(pool_b, 2)[:, 1, :], ALU.add))
            c.link(dve.tensor_tensor(B[:, 1, :], A[:, 1, :], back(pool_a, 4)[:, 1, :], ALU.add))
            c.link(dve.tensor_tensor(A[64:128, 1, :], B[64:128, 1, :], back(pool_b, 8)[64:128, 1, :], ALU.add))
            dve.wait_ge(sem("params_in"), l * 48 + 64)
            c.step(dve.tensor_tensor(pooled[0:64], B[0:64], pool_inv[0:64, :, :], ALU.mult))
            c.link(dve.tensor_tensor(pooled[64:128], A[64:128], pool_inv[64:128, :, :], ALU.mult))
            dve.tensor_tensor(pooled, pooled, u_pool, ALU.subtract).then_inc(sem("pooled"), 1)
            dve.wait_ge(sem("c_sb"), l1)
            now_u, h_bank, b_bank = conv_u[:, :, 2:], bank[5], bank[3]
            c.link(dve.tensor_tensor(now_u, conv_c, h_bank[:, :].rearrange("p (b t) -> p b t", b=2), ALU.mult))
            for b in range(2):
                c.step(dve.tensor_scalar(conv_y[:, b, :], now_u[:, b, :], conv_w[:, 0, b:b + 1], None, ALU.mult))
            c.wait()
            for tap in (1, 2):
                for b in range(2):
                    c.step(dve.scalar_tensor_tensor(conv_y[:, b, :], conv_u[:, b, 2 - tap:2 - tap + T],
                                                    conv_w[:, tap, b:b + 1], conv_y[:, b, :], ALU.mult, ALU.add))
                c.wait()
            dve.tensor_tensor(conv_y, conv_y, b_bank[:, :].rearrange("p (b t) -> p b t", b=2), ALU.mult)\
                .then_inc(sem("conv_y"), 1)
            for u in range(10, 13):
                lo(st, u)
            for b in range(2):
                dve.wait_ge(sem("yT_hi"), l * 5 + 2)
                dve.scalar_tensor_tensor(yT_lo[:, 4 + b, :], bank[2][:, b * T:(b + 1) * T], pool_s[:, b:b + 1],
                                         yT_hi[:, 4 + b, :].bitcast(F32), ALU.mult, ALU.subtract)\
                    .then_inc(sem("yT_lo"), 1)
            dve.wait_ge(sem("yT_hi"), l * 5 + 3)
            dve.wait_ge(sem("conv_y"), l1)
            rest(yT_lo[:, 6:8, :], conv_y, yT_hi[:, 6:8, :]).then_inc(sem("yT_lo"), 1)
            dve.wait_ge(sem("bias_in"), 16 * HEADS)
            for i in range(HEADS + 1):
                if i < HEADS:
                    h = i
                    hold(dve, "logits_mm", l * HEADS + h + 1)
                    if h >= 2:
                        hold(dve, "probT_mm", l * HEADS + h - 1)
                    for t, (a, b, s0) in enumerate(((0, P, P), (P, 3 * P, 0))):
                        c.step(dve.tensor_tensor_reduce(prob[:, h % 2, a:b], bank[6 + h % 2][:, a:b],
                                                        bias[:, h, s0:T], 1.0, 3.0 * MASKED, ALU.add, ALU.max,
                                                        mx[:, h % 2, t:t + 1]))
                    c.wait()
                    dve.tensor_scalar(nmx[:, h % 2, :], mx[:, h % 2, :], -1.0, None, ALU.mult)\
                        .then_inc(sem("logits"), 1)
                if i >= 1:
                    h = i - 1
                    dve.wait_ge(sem("probT_mm"), l * HEADS + h + 1)
                    if h >= 2:
                        dve.wait_ge(sem("pv_mm"), l * HEADS + h - 1)
                    dve.tensor_copy(probT[:, h % 2, 0:3 * P], bank[h % 2][:, 0:3 * P]).then_inc(sem("probT_sb"), 1)
            dve.wait_ge(sem("exp"), l1 * (2 * HEADS))
            c.link(dve.reciprocal(rden[:, :, :], den[:, :, :]))
            dve.wait_ge(sem("pv_mm"), l1 * HEADS)
            for t in range(NT):
                dve.tensor_tensor(y_tok[:, t, :].rearrange("p (h d) -> p h d", h=HEADS),
                                  bank[4 + t][:, :].rearrange("p (h d) -> p h d", h=HEADS),
                                  rden[:, t, :].unsqueeze(2).broadcast_to([P, HEADS, DH]), ALU.mult)\
                    .then_inc(sem("y_tok"), 1)
            for t in range(NT):
                dve.wait_ge(sem("yT_hi"), l * 5 + 4 + t)
                s = (slice(None), slice(0, 4), slice(t * P, (t + 1) * P))
                rest(yT_lo[s], banks4(6 + t), yT_hi[s]).then_inc(sem("yT_lo"), 1)
            for u in range(13, 17):
                lo(st, u)
            add_to_x(st, (12, 13), 0)
            dve.wait_ge(sem("x_ready"), l * 3 + 2)
            norm(l * 3 + 2, x, (0, 1, 2, 3), xT_hi, xT_lo)
            for u in range(17, 20):
                lo(st, u)
            for i in range(XHEADS + 1):
                if i < XHEADS:
                    h = i
                    dve.wait_ge(sem("xlogits_mm"), l * XHEADS + h + 1)
                    if h >= 2:
                        dve.wait_ge(sem("xexp"), (l * XHEADS + h - 1) * NT)
                    c.link(dve.tensor_reduce(mx[:, h % 2, :], bank[6 + h % 2][:, :].rearrange("p (t m) -> p t m", t=NT),
                                             AX.X, ALU.max))
                    dve.tensor_scalar(nmx[:, h % 2, :], mx[:, h % 2, :], -XSCALE, None, ALU.mult)\
                        .then_inc(sem("xmax"), 1)
                if i >= 1:
                    h = i - 1
                    dve.wait_ge(sem("xprobT_mm"), l * XHEADS + h + 1)
                    if h >= 2:
                        dve.wait_ge(sem("xpv_mm"), l * XHEADS + h - 1)
                    dve.tensor_copy(probT[:, h % 2, :], bank[h % 2][:, :]).then_inc(sem("xprobT_sb"), 1)
            dve.wait_ge(sem("xexp"), l1 * (NT * XHEADS))
            c.link(dve.reciprocal(rden[:, :, 0:XHEADS], den[:, :, 0:XHEADS]))
            dve.wait_ge(sem("xpv_mm"), l1 * XHEADS)
            for t in range(NT):
                dve.tensor_tensor(y_tok[:, t, :].rearrange("p (h d) -> p h d", h=XHEADS),
                                  bank[2 + t][:, :].rearrange("p (h d) -> p h d", h=XHEADS),
                                  rden[:, t, 0:XHEADS].unsqueeze(2).broadcast_to([P, XHEADS, XDH]), ALU.mult)\
                    .then_inc(sem("xy_tok"), 1)
            for t in range(NT):
                dve.wait_ge(sem("xyT_hi"), l * 2 + t + 1)
                s = (slice(None), slice(0, 4), slice(t * P, (t + 1) * P))
                rest(yT_lo[s], banks4(4 + t), yT_hi[s]).then_inc(sem("xyT_lo"), 1)
            for u in range(20, 24):
                lo(st, u, 1024)
            add_to_x(st, (21, 23), 0)
            dve.wait_ge(sem("x_ready"), l * 3 + 3)
            norm(l * 3 + 3, x, (4, 5, 6, 7), xT_hi, xT_lo)
            with dve.If(l < 1):
                st = Stream(LAYER_UNITS, LAYER_UNITS // RAW)
                for u in range(4):
                    lo(st, u)
                gate_tiles(FT, NT, 0)
                with dve.Fori(1, DENSE_STEPS) as j:
                    sj = Stream(LAYER_UNITS + (j - 1) * 6, LAYER_UNITS // RAW + (j - 1))
                    lo(sj, 4)
                    lo(sj, 5)
                    hidT_lo(FT, NT, 2, (j - 1) * NT)
                    for u in range(6, 10):
                        lo(sj, u)
                    gate_tiles(FT, NT, j * NT)
                e = 4 + 6 * (DENSE_STEPS - 1)
                lo(st, e, 1024)
                lo(st, e + 1, 1024)
                hidT_lo(FT, NT, 2, (DENSE_STEPS - 1) * NT)
                lo(st, e + 2, 1024)
                lo(st, e + 3, 1024)
                lo(st, e + 4)
                lo(st, e + 5)
                gate_tiles(FT // 2, NT, DENSE_STEPS * NT)
                lo(st, e + 6, 1024)
                hidT_lo(FT // 2, NT, 2, DENSE_STEPS * NT)
                lo(st, e + 7, 1024)
                add_to_x(st, (e + 7, e + 7), 4)
            dve.nop()
        assert c.n == DVE_LAYER, c.n
        c.restart(head + DEPTH * DVE_LAYER)

        dve.wait_ge(sem("router_in"), 32)
        dve.wait_ge(sem("router_hi"), 1)
        rest(router_lo[:, :, :], router[:, :, :], router_hi[:, :, :]).then_inc(sem("router_lo"), 1)
        dve.wait_ge(sem("router_mm"), 1)

        def over_experts(ap):
            return ap.unsqueeze(2).broadcast_to([P, NT, NE])

        c.link(dve.tensor_copy(lg[:, :, :], bank[0][:, 0:NT * NE].rearrange("p (t e) -> p t e", t=NT)))

        def pick_first(best, place, out):
            c.link(dve.tensor_reduce(best, lg[:, :, :], AX.X, ALU.max))
            c.link(dve.tensor_tensor(tmp8[:, :, :], lg[:, :, :], over_experts(best), ALU.is_equal))
            c.link(dve.tensor_tensor(tmp8[:, :, :], tmp8[:, :, :], less8[:, :, :], ALU.mult))
            c.link(dve.tensor_reduce(place, tmp8[:, :, :], AX.X, ALU.min))
            c.link(dve.tensor_tensor(out, less8[:, :, :], over_experts(place), ALU.is_equal))

        pick_first(top[:, 0, :], top[:, 3, :], sel1[:, :, :])
        c.link(dve.scalar_tensor_tensor(lg[:, :, :], sel1[:, :, :], -3e38, lg[:, :, :], ALU.mult, ALU.add))
        pick_first(top[:, 4, :], top[:, 5, :], sel2[:, :, :])
        dve.tensor_tensor(top[:, 1, :], top[:, 4, :], top[:, 0, :], ALU.subtract).then_inc(sem("top_diff"), 1)
        dve.tensor_tensor(mask[:, :, :], sel1[:, :, :], sel2[:, :, :], ALU.add).then_inc(sem("mask"), 1)
        dve.wait_ge(sem("top_exp"), 1)
        c.link(dve.tensor_scalar(top[:, 6, :], top[:, 2, :], 1.0, None, ALU.add))
        c.link(dve.reciprocal(top[:, 7, :], top[:, 6, :]))
        c.link(dve.tensor_tensor(top[:, 6, :], top[:, 2, :], top[:, 7, :], ALU.mult))
        c.step(dve.tensor_tensor(sel1[:, :, :], sel1[:, :, :], over_experts(top[:, 7, :]), ALU.mult))
        c.link(dve.tensor_tensor(sel2[:, :, :], sel2[:, :, :], over_experts(top[:, 6, :]), ALU.mult))
        c.link(dve.tensor_tensor(gates[:, :, :], sel1[:, :, :], sel2[:, :, :], ALU.add))
        dve.wait_ge(sem("rank_mm"), 1)
        dve.wait_ge(sem("mask"), 1)
        rank = bank[1][:, 0:NT * NE].rearrange("p (t e) -> p t e", t=NT)
        c.link(dve.scalar_tensor_tensor(tmp8[:, :, :], rank, 1.0, mask[:, :, :], ALU.add, ALU.mult))
        c.link(dve.tensor_scalar(tmp8[:, :, :], tmp8[:, :, :], -1.0, None, ALU.add))
        c.step(dve.tensor_copy(places[:, 0:NE, 0, :].rearrange("p e t -> p t e"), tmp8[:, :, :]))
        c.step(dve.tensor_copy(places[:, 0:NE, 1, :].rearrange("p e t -> p t e"), gates[:, :, :]))
        c.link(dve.tensor_scalar(over[:, :], bank[1][:, 2 * NE:3 * NE], float(P), None, ALU.is_gt))
        c.link(dve.tensor_reduce(first[:, 0:1], over[:, :], AX.X, ALU.add))
        c.link(dve.tensor_scalar(first[:, 0:1], first[:, 0:1], float(NE), None, ALU.add))
        c.link(dve.tensor_scalar(lg[:, :, :], tmp8[:, :, :], -float(P - 1), None, ALU.add))
        for k in range(OVER):
            c.link(dve.tensor_tensor(pick[:, k, :], over[:, :], less8[:, 0, :], ALU.mult))
            c.link(dve.tensor_reduce(first[:, k + 1:k + 2], pick[:, k, :], AX.X, ALU.min))
            c.link(dve.tensor_scalar(pick[:, k, :], less8[:, 0, :], first[:, k + 1:k + 2], None, ALU.is_equal))
            c.link(dve.tensor_tensor(over[:, :], over[:, :], pick[:, k, :], ALU.subtract))
            picked = pick[:, k, :].unsqueeze(1).broadcast_to([P, NT, NE])
            c.link(dve.tensor_tensor(tmp8[:, :, :], lg[:, :, :], picked, ALU.mult))
            c.link(dve.tensor_reduce(top[:, 0, :], tmp8[:, :, :], AX.X, ALU.add))
            c.step(dve.tensor_scalar(places[:, NE + k, 0, :], top[:, 0, :], -1.0, None, ALU.add))
            c.link(dve.tensor_tensor(tmp8[:, :, :], gates[:, :, :], picked, ALU.mult))
            c.link(dve.tensor_reduce(places[:, NE + k, 1, :], tmp8[:, :, :], AX.X, ALU.add))
        c.link(dve.tensor_scalar(first[:, 1:OVER + 1], first[:, 1:OVER + 1], float(NE), float(NE - 1), ALU.add, ALU.min))
        dve.tensor_copy(info[0:1, :], first[0:1, :]).then_inc(sem("info_ready"), 1)
        dve.wait_ge(sem("info_ready"), 1)
        n_items = dve.value_load(info[0:1, 0:1], min_val=NE, max_val=ITEMS)

        def select(out, places_of, with_gate):
            for t in range(NT):
                if with_gate:
                    last = dve.tensor_scalar(out[:, t, :], iota, places_of[:, 0, t:t + 1], places_of[:, 1, t:t + 1],
                                             ALU.is_equal, ALU.mult)
                else:
                    last = dve.tensor_scalar(out[:, t, :], iota, places_of[:, 0, t:t + 1], None, ALU.is_equal)
            return last

        def gathered_lo(i):
            for b in range(2):
                dve.wait_ge(sem("gather_hi"), i * 2 + b + 1)
                rest(xgT_lo[:, 4 * b:4 * b + 4, :], banks4(6 + b), xgT_hi[:, 4 * b:4 * b + 4, :])\
                    .then_inc(sem("gather_lo"), 1)

        def add_rows(i):
            for n in range(4):
                t, s = n // 2, slice(n % 2 * 512, (n % 2 + 1) * 512)
                dve.wait_ge(sem("scatter_mm"), i * 4 + n + 1)
                dve.tensor_tensor(x[:, t, s], x[:, t, s], bank[SCATTER[n]][:, :], ALU.add)\
                    .then_inc(sem("scatter_add"), 1)

        dve.wait_ge(sem("dve_step"), head + DEPTH * DVE_LAYER + c.n)
        select(S, places[:, 0, :, :], False).then_inc(sem("select"), 1)
        dve.sem_inc(sem("SgT"), 1)
        gathered_lo(0)
        routed = head + DEPTH * DVE_LAYER + c.n
        MO = DENSE_STEPS + 1
        MT = NT * MO
        ITEM_CHAIN = 1
        with dve.Fori(0, ITEMS) as i:
            with dve.If(n_items > i):
                c.restart(i * ITEM_CHAIN + routed)
                st = Stream(i * ITEM_UNITS + MOE_BASE, i * (ITEM_UNITS // RAW) + MOE_BASE // RAW)
                for u in range(3):
                    lo(st, u)
                with dve.If(i > 0):
                    add_rows(i)
                lo(st, 3)
                gate_tiles(FT, 1, i * ITEM_STEPS + MT)
                c.link(dve.tensor_copy(now[:, :, :, :], places[:, bass.ds(i, 2), :, :]))
                select(Sg, now[:, 0, :, :], True).then_inc(sem("select_gated"), 1)
                dve.wait_ge(sem("gather_mm"), i * 2 + 2)
                select(S, now[:, 1, :, :], False).then_inc(sem("select"), 1)
                with dve.Fori(1, ITEM_STEPS) as j:
                    sj = Stream(i * ITEM_UNITS + (j - 1) * 6 + MOE_BASE,
                                i * (ITEM_UNITS // RAW) + (j - 1) + MOE_BASE // RAW)
                    lo(sj, 4)
                    lo(sj, 5)
                    hidT_lo(FT, 1, 2, i * ITEM_STEPS + (j - 1) + MT)
                    for u in range(6, 10):
                        lo(sj, u)
                    gate_tiles(FT, 1, i * ITEM_STEPS + j + MT)
                e = 4 + 6 * (ITEM_STEPS - 1)
                lo(st, e)
                lo(st, e + 1)
                hidT_lo(FT, 1, 2, i * ITEM_STEPS + (ITEM_STEPS - 1) + MT)
                dve.wait_ge(sem("select_mm"), i + 1)
                dve.tensor_copy(SgT[:, :, :], bank[1][:, 0:NT * P].rearrange("p (t r) -> p t r", t=NT))\
                    .then_inc(sem("SgT"), 1)
                gathered_lo(i + 1)
            dve.nop()
        add_rows(n_items)
        hold(dve, "scatter_add", n_items * 4)
        dve.sem_inc(sem("x_final"), 1)
        c.restart(n_items * ITEM_CHAIN + routed)
        norm(3 * DEPTH + 1, x, None, None, None)

    @block.tensor
    def _(pe):
        def passes(out, hi_l, lo_l, hi_r, lo_r, start, stop):
            pe.matmul(out, hi_l, hi_r, start=start, stop=False, skip_group_check=True)
            pe.matmul(out, hi_l, lo_r, start=False, stop=False, skip_group_check=True)
            return pe.matmul(out, lo_l, hi_r, start=False, stop=stop, skip_group_check=True)

        def halves(st, u):
            for half in range(2):
                pe.wait_ge(sem("raw_free"), st.upto(u, half) + 2 * RAW)
                yield half, w_hi[:, u % SPLIT, half, :], w_lo[:, u % SPLIT, half, :]

        def tokens_out(st, u, kn, width, xs, banks, first, last):
            x_hi, x_lo, k_x = xs
            n = kn // 2
            for half, h, lo_ in halves(st, u):
                for t, b in enumerate(banks):
                    for k in range(n):
                        s, r = slice(k * width, (k + 1) * width), slice(t * P, (t + 1) * P)
                        kx = k_x + half * n + k
                        mm = passes(bank[b][:, 0:width], x_hi[:, kx, r], x_lo[:, kx, r], h[:, s], lo_[:, s],
                                    first and half == 0 and k == 0, last and half == 1 and k == n - 1)
                mm.then_inc(sem("unit_used"), 1)

        def features_out(st, u, k0, xs, banks, first, last):
            x_hi, x_lo = xs
            for half, h, lo_ in halves(st, u):
                for cb in range(4):
                    out = bank[banks[cb // 2]][:, (cb % 2) * T:(cb % 2) * T + T]
                    for k in range(2):
                        s, kx = slice(k * 512 + cb * P, k * 512 + (cb + 1) * P), k0 + 2 * half + k
                        mm = passes(out, h[:, s], lo_[:, s], x_hi[:, kx, :], x_lo[:, kx, :],
                                    first and half == 0 and k == 0 and cb % 2 == 0, last and half == 1 and k == 1)
                mm.then_inc(sem("unit_used"), 1)

        def norm(m, banks):
            for t in range(NT):
                pe.wait_ge(sem("xn_ready"), m * NT + t + 1)
                for half in range(2):
                    for k in range(4):
                        a = (4 * half + k) * P
                        mm = pe.transpose(bank[banks[2 * t + half]][:, k * P:(k + 1) * P], xn[:, t, a:a + P], ident)
                    mm.then_inc(sem("xT_mm"), 1)

        pe.sem_inc(sem("scatter_mm"), 4)
        pe.sem_inc(sem("unit_used"), 2 * SPLIT)
        pe.wait_ge(sem("mats_in"), 16)
        pe.wait_ge(sem("zeros"), 1)
        pe.wait_ge(sem("table_in"), 32)
        for h in range(HEADS):
            pe.matmul(bank[h][:, 0:SKEW_W], rel[:, h:h + 1].broadcast_to([BUCKETS + 1, P]), table[:, :],
                      start=True, stop=True).then_inc(sem("skew_mm"), 1)
        pe.wait_ge(sem("skew_rows"), HEADS)
        norm(0, (0, 1, 2, 3))

        with pe.Fori(0, DEPTH) as l:
            l1 = l + 1
            st = Stream(l * (LAYER_UNITS + DENSE_UNITS), l * ((LAYER_UNITS + DENSE_UNITS) // RAW))
            xs = (xT_hi, xT_lo)
            pe.wait_ge(sem("xT_lo"), l * 12 + 4)
            norm(l * 3 + 1, (0, 1, 2, 3))
            pe.wait_ge(sem("xT_lo"), l * 12 + 8)
            features_out(st, 0, 0, xs, (4, 5), True, False)
            features_out(st, 1, 4, xs, (4, 5), False, True)
            features_out(st, 2, 0, xs, (6, 7), True, False)
            features_out(st, 3, 4, xs, (6, 7), False, True)
            tokens_out(st, 4, 4, 512, (xT_hi, xT_lo, 0), (0, 1), True, False)
            tokens_out(st, 5, 4, 512, (xT_hi, xT_lo, 4), (0, 1), False, True)
            features_out(st, 6, 0, xs, (2, 3), True, False)
            features_out(st, 7, 4, xs, (2, 3), False, True)
            pe.wait_ge(sem("q_sb"), l1 * 2)
            features_out(st, 8, 0, xs, (4, 5), True, False)
            features_out(st, 9, 4, xs, (4, 5), False, True)
            hold(pe, "params_in", l * 48 + 64)
            hold(pe, "pooled", l1)
            for b in range(2):
                for g in range(2):
                    r = slice(g * 64, g * 64 + 64)
                    mm = pe.matmul(bank[2][r, b * T:(b + 1) * T], pool_w[r, b, :], pooled[r, b, :],
                                   start=True, stop=True)
            mm.then_inc(sem("pool_mm"), 1)
            pe.wait_ge(sem("k_sb"), l1 * 2)
            pe.wait_ge(sem("v_sb"), l1 * 2)
            pe.wait_ge(sem("conv_y"), l1)
            for i in range(HEADS + 2):
                if i < HEADS:
                    h = i
                    if h >= 2:
                        pe.wait_ge(sem("logits"), l * HEADS + h - 1)
                    r = slice((h % 2) * 64, (h % 2) * 64 + 64)
                    pe.matmul(bank[6 + h % 2][:, 0:P], qk[r, 0, h // 2, 0:P], qk[r, 1, h // 2, 0:P],
                              start=True, stop=True)
                    pe.matmul(bank[6 + h % 2][:, P:3 * P], qk[r, 0, h // 2, P:T], qk[r, 1, h // 2, :],
                              start=True, stop=True).then_inc(sem("logits_mm"), 1)
                if 1 <= i <= HEADS:
                    h = i - 1
                    pe.wait_ge(sem("exp"), (l * HEADS + h + 1) * 2)
                    if h >= 2:
                        pe.wait_ge(sem("probT_sb"), l * HEADS + h - 1)
                    for b in range(3):
                        mm = pe.transpose(bank[h % 2][:, b * P:(b + 1) * P], prob[:, h % 2, b * P:(b + 1) * P], ident)
                    mm.then_inc(sem("probT_mm"), 1)
                if i >= 2:
                    h = i - 2
                    pe.wait_ge(sem("probT_sb"), l * HEADS + h + 1)
                    d = slice(h * DH, (h + 1) * DH)
                    pe.matmul(bank[4][:, d], probT[:, h % 2, 0:P], v[:, 0, d], start=True, stop=True)
                    pe.matmul(bank[5][:, d], probT[:, h % 2, P:2 * P], v[:, 0, d], start=True, stop=False)
                    pe.matmul(bank[5][:, d], probT[:, h % 2, 2 * P:3 * P], v[:, 1, d], start=False, stop=True)\
                        .then_inc(sem("pv_mm"), 1)
            pe.wait_ge(sem("logits"), l1 * HEADS)
            for t in range(NT):
                pe.wait_ge(sem("y_tok"), l * 2 + t + 1)
                for k in range(4):
                    mm = pe.transpose(bank[6 + t][:, k * P:(k + 1) * P], y_tok[:, t, k * P:(k + 1) * P], ident)
                mm.then_inc(sem("yTok_mm"), 1)
            pe.wait_ge(sem("yT_lo"), l * 5 + 3)
            tokens_out(st, 10, 4, 512, (yT_hi, yT_lo, 4), (0, 1), True, False)
            tokens_out(st, 11, 4, 512, (yT_hi, yT_lo, 4), (2, 3), True, False)
            pe.wait_ge(sem("yT_lo"), l * 5 + 5)
            tokens_out(st, 12, 4, 512, (yT_hi, yT_lo, 0), (0, 1), False, True)
            tokens_out(st, 13, 4, 512, (yT_hi, yT_lo, 0), (2, 3), False, True)
            ms = (memT_hi, memT_lo)
            features_out(st, 14, 0, ms, (4, 5), True, False)
            features_out(st, 15, 4, ms, (4, 5), False, True)
            tokens_out(st, 16, 4, 512, (memT_hi, memT_lo, 0), (6, 7), True, False)
            norm(l * 3 + 2, (0, 1, 2, 3))
            tokens_out(st, 17, 4, 512, (memT_hi, memT_lo, 4), (6, 7), False, True)
            pe.wait_ge(sem("xT_lo"), l * 12 + 12)
            pe.wait_ge(sem("xk_sb"), l1 * 2)
            features_out(st, 18, 0, xs, (4, 5), True, False)
            features_out(st, 19, 4, xs, (4, 5), False, True)
            pe.wait_ge(sem("xv_sb"), l1 * 2)
            pe.wait_ge(sem("xq_sb"), l1 * 2)
            for i in range(XHEADS + 2):
                if i < XHEADS:
                    h = i
                    if h >= 2:
                        pe.wait_ge(sem("xexp"), (l * XHEADS + h - 1) * 2)
                    for t in range(NT):
                        mm = pe.matmul(bank[6 + h % 2][:, t * T:(t + 1) * T], qk[:, 0, h, t * P:(t + 1) * P],
                                       qk[:, 1, h, :], start=True, stop=True)
                    mm.then_inc(sem("xlogits_mm"), 1)
                if 1 <= i <= XHEADS:
                    h = i - 1
                    pe.wait_ge(sem("xexp"), (l * XHEADS + h + 1) * 2)
                    if h >= 2:
                        pe.wait_ge(sem("xprobT_sb"), l * XHEADS + h - 1)
                    for b in range(4):
                        mm = pe.transpose(bank[h % 2][:, b * P:(b + 1) * P], prob[:, h % 2, b * P:(b + 1) * P], ident)
                    mm.then_inc(sem("xprobT_mm"), 1)
                if i >= 2:
                    h = i - 2
                    pe.wait_ge(sem("xprobT_sb"), l * XHEADS + h + 1)
                    d = slice(h * XDH, (h + 1) * XDH)
                    for t in range(NT):
                        for b in range(2):
                            a = (2 * t + b) * P
                            mm = pe.matmul(bank[2 + t][:, d], probT[:, h % 2, a:a + P], v[:, b, d],
                                           start=(b == 0), stop=(b == 1))
                    mm.then_inc(sem("xpv_mm"), 1)
            for t in range(NT):
                pe.wait_ge(sem("xy_tok"), l * 2 + t + 1)
                for k in range(4):
                    mm = pe.transpose(bank[4 + t][:, k * P:(k + 1) * P], y_tok[:, t, k * P:(k + 1) * P], ident)
                mm.then_inc(sem("xyT_mm"), 1)
            pe.wait_ge(sem("xyT_lo"), l1 * 2)
            for n in range(4):
                tokens_out(st, 20 + n, 2, 512, (yT_hi, yT_lo, 2 * (n % 2)), (2 * (n // 2), 2 * (n // 2) + 1),
                           n % 2 == 0, n % 2 == 1)
            norm(l * 3 + 3, (4, 5, 6, 7))
            pe.wait_ge(sem("xT_lo"), l * 12 + 16)

            def up(st, u, ks, width, xs, banks):
                for m in range(2):
                    if m == 1 and ks is not None:
                        ks()
                    tokens_out(st, u + m, 4, width, (xs[0], xs[1], 4 * m), banks, m == 0, m == 1)

            def turn(width, tiles):
                for t in range(tiles):
                    for k in range(width // P):
                        mm = pe.transpose(bank[2 + t][:, k * P:(k + 1) * P], hid[:, t, k * P:(k + 1) * P], ident)
                mm.then_inc(sem("hidT_mm"), 1)

            def down(st, u, tiles, short=False, last=False):
                for m in range(2):
                    for half, h, lo_ in halves(st, u + m):
                        k = m if short else 2 * m + half
                        for t in range(tiles):
                            r = slice(t * P, (t + 1) * P)
                            for col in ((half,) if short else (0, 1)):
                                s = slice(0, 512) if short else slice(col * 512, (col + 1) * 512)
                                b = bank[4 + (2 * col + t if tiles == 2 else col)]
                                mm = passes(b[:, :], yT_hi[:, k, r], yT_lo[:, k, r], h[:, s], lo_[:, s],
                                            False, last and m == 1 and (short or half == 1))
                        mm.then_inc(sem("unit_used"), 1)

            def clear(banks):
                for b in banks:
                    pe.matmul(bank[b][:, :], zeros[:, 0:P], zeros[:, :], start=True, stop=False, skip_group_check=True)

            with pe.If(l < 1):
                st = Stream(LAYER_UNITS, LAYER_UNITS // RAW)
                clear((4, 5, 6, 7))
                up(st, 0, None, FT, xs, (0, 1))
                up(st, 2, None, FT, xs, (2, 3))
                with pe.Fori(1, DENSE_STEPS) as j:
                    sj = Stream(LAYER_UNITS + (j - 1) * 6, LAYER_UNITS // RAW + (j - 1))
                    pe.wait_ge(sem("hid_ready"), j * NT)
                    up(sj, 4, lambda: turn(FT, NT), FT, xs, (0, 1))
                    pe.wait_ge(sem("hidT_lo"), j * NT)
                    up(sj, 6, None, FT, xs, (2, 3))
                    down(sj, 8, NT)
                e = 4 + 6 * (DENSE_STEPS - 1)
                pe.wait_ge(sem("hid_ready"), DENSE_STEPS * NT)
                up(st, e, lambda: turn(FT, NT), FT // 2, xs, (0, 1))
                pe.wait_ge(sem("hidT_lo"), DENSE_STEPS * NT)
                up(st, e + 2, None, FT // 2, xs, (2, 3))
                down(st, e + 4, NT)
                pe.wait_ge(sem("hid_ready"), (DENSE_STEPS + 1) * NT)
                turn(FT // 2, NT)
                pe.wait_ge(sem("hidT_lo"), (DENSE_STEPS + 1) * NT)
                down(st, e + 6, NT, short=True, last=True)
            pe.nop()

        pe.wait_ge(sem("router_lo"), 1)
        for t in range(NT):
            out, r = bank[0][:, t * NE:(t + 1) * NE], slice(t * P, (t + 1) * P)
            for k in range(KD):
                passes(out, xT_hi[:, k, r], xT_lo[:, k, r], router_hi[:, k, :], router_lo[:, k, :],
                       k == 0, False)
                mm = pe.matmul(out, xT_lo[:, k, r], router_lo[:, k, :], start=False, stop=(k == KD - 1),
                               skip_group_check=True)
        mm.then_inc(sem("router_mm"), 1)
        pe.wait_ge(sem("mask"), 1)
        pe.matmul(bank[1][:, 0:NE], before, mask[:, 0, :], start=True, stop=True)
        pe.matmul(bank[1][:, NE:2 * NE], ones, mask[:, 0, :], start=True, stop=False)
        pe.matmul(bank[1][:, NE:2 * NE], before, mask[:, 1, :], start=False, stop=True)
        pe.matmul(bank[1][:, 2 * NE:3 * NE], ones, mask[:, 0, :], start=True, stop=False)
        pe.matmul(bank[1][:, 2 * NE:3 * NE], ones, mask[:, 1, :], start=False, stop=True).then_inc(sem("rank_mm"), 1)
        pe.wait_ge(sem("info_ready"), 1)
        n_items = pe.value_load(info[0:1, 0:1], min_val=NE, max_val=ITEMS)

        def gather(i):
            pe.wait_ge(sem("select"), i + 1)
            for b in range(2):
                for k in range(4):
                    a = (4 * b + k) * P
                    for t in range(NT):
                        mm = pe.matmul(bank[6 + b][:, k * P:(k + 1) * P], xn[:, t, a:a + P], S[:, t, :],
                                       start=(t == 0), stop=(t == NT - 1))
                mm.then_inc(sem("gather_mm"), 1)

        def scatter(i):
            pe.wait_ge(sem("rows_sb"), i * 2 + 2)
            pe.wait_ge(sem("SgT"), i + 1)
            for n in range(4):
                t, col = n // 2, n % 2
                pe.matmul(bank[SCATTER[n]][:, :], SgT[:, t, :], y_sb[:, col * 512:(col + 1) * 512],
                          start=True, stop=True).then_inc(sem("scatter_mm"), 1)

        gather(0)
        MO = DENSE_STEPS + 1
        MT = NT * MO
        gs = (xgT_hi, xgT_lo)
        with pe.Fori(0, ITEMS) as i:
            with pe.If(n_items > i):
                st = Stream(i * ITEM_UNITS + MOE_BASE, i * (ITEM_UNITS // RAW) + MOE_BASE // RAW)
                pe.wait_ge(sem("gather_lo"), i * 2 + 2)
                up(st, 0, None, FT, gs, (0,))
                with pe.If(i > 0):
                    scatter(i)
                clear((4, 5))
                up(st, 2, None, FT, gs, (2,))
                with pe.Fori(1, ITEM_STEPS) as j:
                    sj = Stream(i * ITEM_UNITS + (j - 1) * 6 + MOE_BASE,
                                i * (ITEM_UNITS // RAW) + (j - 1) + MOE_BASE // RAW)
                    pe.wait_ge(sem("hid_ready"), i * ITEM_STEPS + j + MT)
                    up(sj, 4, lambda: turn(FT, 1), FT, gs, (0,))
                    pe.wait_ge(sem("hidT_lo"), i * ITEM_STEPS + j + MT)
                    up(sj, 6, None, FT, gs, (2,))
                    down(sj, 8, 1)
                pe.wait_ge(sem("hid_ready"), i * ITEM_STEPS + ITEM_STEPS + MT)
                turn(FT, 1)
                pe.wait_ge(sem("select_gated"), i + 1)
                for t in range(NT):
                    mm = pe.transpose(bank[1][:, t * P:(t + 1) * P], Sg[:, t, :], ident)
                mm.then_inc(sem("select_mm"), 1)
                gather(i + 1)
                pe.wait_ge(sem("hidT_lo"), i * ITEM_STEPS + ITEM_STEPS + MT)
                down(st, 4 + 6 * (ITEM_STEPS - 1), 1, last=True)
            pe.nop()
        pe.wait_ge(sem("gather_lo"), n_items * 2 + 2)
        scatter(n_items)


_INPUTS = ("x", "mem", "rel_bias", "mem_norm_g", "mix_norm_g", "w_in", "conv_w", "pool_w", "pool_scale", "w_out",
           "xattn_norm_g", "wq_x", "wkv_x", "wo_x", "ffn_norm_g", "w13_dense", "w2_dense", "router_w", "w13_moe",
           "w2_moe", "final_norm_g")


def kernel(**inputs):
    import concourse.bacc as bacc
    from concourse.bass_utils import run_bass_kernel_spmd

    nc = bacc.Bacc("TRN2", target_bir_lowering=False, num_devices=1)
    arrays, io = {}, {}
    given = {name: np.ascontiguousarray(inputs[name]) for name in _INPUTS}
    given.update(shape_constants())
    for name, a in given.items():
        arrays[f"in_{name}"] = a
        io[name] = nc.dram_tensor(f"in_{name}", a.shape, mybir.dt.from_np(a.dtype), kind="ExternalInput").ap()
    io["out"] = nc.dram_tensor("out", (1, T, D), F32, kind="ExternalOutput").ap()
    build(nc, io)
    r = run_bass_kernel_spmd(nc, [arrays], core_ids=[0])
    return r.results[0]["out"]
```

```python
from contextlib import ExitStack

import numpy as np

import concourse.bass as bass
from concourse import mybir

F32, F32R, I32, BF16 = mybir.dt.float32, mybir.dt.float32r, mybir.dt.int32, mybir.dt.bfloat16
ACT = mybir.ActivationFunctionType
ALU = mybir.AluOpType
AX = mybir.AxisListType

P = 128
D = 1024
KD = D // P
T = 256
NT = T // P
DEPTH = 2
EPS = 1e-6

HEADS, DH = 8, 64
PAIRS = HEADS // 2
WINDOWS = ((128, 1), (512, 4), (2048, 16))
BUCKETS, MAX_DIST = 32, 128
MASKED = -1e30

XHEADS, XDH = 4, 128
XSCALE = XDH ** -0.5
IN_W = 2560

FD = 2816
FE = 3584
NE = 8
OVER = 3
ITEMS = NE + OVER

FT = 512
UNIT = 2048
RAW = 6
SPLIT = 3

LAYER_UNITS = 24
DENSE_UNITS = 36
ITEM_UNITS = 6 * (FE // FT)
DENSE_STEPS = FD // FT
DENSE_TURNS = DENSE_STEPS + 1
ITEM_STEPS = FE // FT
MOE_BASE = DEPTH * LAYER_UNITS + DENSE_UNITS

DVE_LAYER = 37
ITEM_CHAIN = 1

SKEW_W = 384


def _bucket(dist):
    exact = BUCKETS // 2
    d = np.maximum(dist, 1).astype(np.float32)
    large = exact + (np.log(d / exact) / np.log(MAX_DIST / exact) * (BUCKETS - exact)).astype(np.int32)
    large = np.minimum(large, BUCKETS - 1)
    return np.where(dist < exact, dist, large).astype(np.int32)


def shape_constants():
    table = np.zeros((BUCKETS + 1, SKEW_W), np.float32)
    for i in range(SKEW_W):
        dist = T - 1 - i
        reach = sum(1 for w, d in WINDOWS if 0 <= dist <= w and dist % d == 0) if dist >= 0 else 0
        if reach:
            table[int(_bucket(np.array(dist))), i] = 1.0
            table[BUCKETS, i] = np.log(float(reach))
        else:
            table[BUCKETS, i] = MASKED
    inv = np.zeros((P, 2, T), np.float32)
    for g, w in enumerate((2, 4, 8, 16)):
        inv[(g % 2) * 64:(g % 2) * 64 + 64, g // 2, :] = 1.0 / np.minimum(np.arange(1, T + 1), w)
    mats = np.zeros((P, 4, P), np.float32)
    mats[:, 0, :] = np.eye(P)
    mats[:, 1, :] = np.triu(np.ones((P, P)), 1)
    mats[:, 2, :] = 1.0
    mats[:, 3, :] = np.arange(P)[None, :]
    less8 = np.tile(np.arange(NE, dtype=np.float32) - NE, (P, NT, 1))
    return {"bias_table": table, "pool_inv": inv, "mats": mats, "less8": less8}


class Chain:

    def __init__(self, eng, sem):
        self.eng, self.sem, self.base, self.n = eng, sem, 0, 0

    def step(self, ins):
        ins.then_inc(self.sem, 1)
        self.n += 1
        return ins

    def wait(self):
        self.eng.wait_ge(self.sem, self.base + self.n)

    def link(self, ins):
        self.step(ins)
        self.wait()

    def restart(self, base):
        self.base, self.n = base, 0


class Stream:

    def __init__(self, first, rounds):
        self.halves, self.rounds = first * 2, rounds

    def upto(self, u, half=1):
        return self.halves + (2 * u + half + 1)

    def landed(self, u):
        return (self.rounds + (u // RAW + 1)) * 16


def build(nc, io):
    with ExitStack() as ctx:
        _build(nc, io, ctx)


def _build(nc, io, ctx):
    def sb(name, shape, dt=F32):
        return ctx.enter_context(nc.sbuf_tensor(name, shape, dt))

    sems = {}

    def sem(name):
        if name not in sems:
            sems[name] = ctx.enter_context(nc.semaphore(name))
        return sems[name]

    raw = sb("raw", [P, RAW, UNIT])
    w_hi = sb("w_hi", [P, SPLIT, 2, UNIT // 2], F32R)
    w_lo = sb("w_lo", [P, SPLIT, 2, UNIT // 2], F32R)
    x = sb("x", [P, NT, D])
    xn = sb("xn", [P, NT, D])
    xT_hi = sb("xT_hi", [P, KD, T], F32R)
    xT_lo = sb("xT_lo", [P, KD, T], F32R)
    memT_hi = sb("memT_hi", [P, KD, T], F32R)
    memT_lo = sb("memT_lo", [P, KD, T], F32R)
    yT_hi = sb("yT_hi", [P, KD, T], F32R)
    yT_lo = sb("yT_lo", [P, KD, T], F32R)
    g_row = sb("g_row", [P, D])
    bias = sb("bias", [P, HEADS, T])
    qk = sb("qk", [P, 2, PAIRS, T])
    v = sb("v", [P, NT, 512])
    prob = sb("prob", [P, 2, 512])
    probT = sb("probT", [P, 2, 512])
    conv_u = sb("conv_u", [P, 2, T + 2])
    pool_a = sb("pool_a", [P, 2, T + 16])
    pool_b = sb("pool_b", [P, 2, T + 16])
    pool_inv = sb("pool_inv", [P, 2, T])
    mats = sb("mats", [P, 4, P])
    zeros = sb("zeros", [P, 512], BF16)
    conv_w = sb("conv_w", [P, 3, 2])
    pool_w = sb("pool_w", [P, 2, 64])
    pool_s = sb("pool_s", [P, 2])
    rel = sb("rel", [BUCKETS + 1, HEADS])
    eps_col = sb("eps_col", [P, 1])
    ss = sb("ss", [P, NT])
    lnv = sb("lnv", [P, NT])
    r0 = sb("r0", [P, NT])
    nw = sb("nw", [P, 3, NT])
    rstd = sb("rstd", [P, NT])
    mx = sb("mx", [P, 2, NT])
    nmx = sb("nmx", [P, 2, NT])
    den = sb("den", [P, NT, HEADS])
    rden = sb("rden", [P, NT, HEADS])
    router = sb("router", [P, KD, NE])
    router_parts = sb("router_parts", [P, KD, 2 * NE], F32R)
    lg_lo = sb("lg_lo", [P, NT, NE])
    less8 = sb("less8", [P, NT, NE])
    lg = sb("lg", [P, NT, NE])
    tmp8 = sb("tmp8", [P, NT, NE])
    sel1 = sb("sel1", [P, NT, NE])
    sel2 = sb("sel2", [P, NT, NE])
    mask = sb("mask", [P, NT, NE])
    gates = sb("gates", [P, NT, NE])
    top = sb("top", [P, 8, NT])
    over = sb("over", [P, NE])
    pick = sb("pick", [P, OVER, NE])
    first = sb("first", [P, OVER + 1])
    places = sb("places", [P, ITEMS + 1, 2, NT])
    now = sb("now", [P, 2, 2, NT])
    info = sb("info", [1, OVER + 1], I32)
    parts_sb = probT[0:2 * NE, 1, 0:T]
    S = prob[:, 0, 0:NT * P].rearrange("p (t r) -> p t r", t=NT)
    Sg = prob[:, 1, 0:NT * P].rearrange("p (t r) -> p t r", t=NT)
    SgT = probT[:, 0, 0:NT * P].rearrange("p (t r) -> p t r", t=NT)

    bank = [ctx.enter_context(nc.psum_tensor(f"bank{i}", [P, 512], F32)) for i in range(8)]
    skew = nc.dram_tensor("skew", [HEADS, P, SKEW_W], F32, kind="Internal")

    ident = mats[:, 0, :]
    before = mats[:, 1, :]
    ones = mats[:, 2, :]
    iota = mats[:, 3, :]
    xn_flat = xn[:, :, :].rearrange("p t d -> p (t d)")
    qk_flat = qk[:, :, :, :].rearrange("p a b t -> p (a b t)")
    mem_sb = bias[:, :, :].rearrange("p h c -> p (h c)").rearrange("p (t d) -> p t d", t=NT)
    table = probT[0:BUCKETS + 1, 0, 0:SKEW_W]
    skew_rows = prob[0:HEADS, 0, 0:SKEW_W]
    conv_c = xn_flat[:, 0:512].rearrange("p (b t) -> p b t", b=2)
    conv_y = xn_flat[:, 512:1024].rearrange("p (b t) -> p b t", b=2)
    pooled = xn_flat[:, 1024:1536].rearrange("p (b t) -> p b t", b=2)
    y_tok = xn_flat[:, 0:1024].rearrange("p (t f) -> p t f", t=NT)
    hid = qk_flat[:, 0:1024].rearrange("p (t f) -> p t f", t=NT)
    y_sb = qk_flat[:, 1024:2048]
    xgT_hi = yT_hi[:, 4:8, :].rearrange("p k t -> p (k t)").rearrange("p (k r) -> p k r", k=KD)
    xgT_lo = yT_lo[:, 4:8, :].rearrange("p k t -> p (k t)").rearrange("p (k r) -> p k r", k=KD)

    def banks4(b):
        return bank[b][:, :].rearrange("p (k t) -> p k t", t=P)

    SCATTER = (3, 1, 6, 7)
    block = ctx.enter_context(nc.Block())

    def used(eng, st, u):
        eng.wait_ge(sem("unit_used"), st.upto(u) + 2 * SPLIT)

    def hold(eng, name, count):
        eng.wait_ge(sem(name), count)
        eng.sem_inc(sem("held"), 1)

    @block.sync
    def _(sp):
        def load(st, u, src, width=UNIT):
            hold(sp, "raw_free", st.upto(u))
            dst = raw[:, u % RAW, 0:width]
            n = src.shape[-1]
            sp.dma_start(dst.rearrange("p (k c) -> p k c", c=n), src).then_inc(sem(f"raw{u % RAW}"), 16)

        def rows(w, k0, kn, c0, cn):
            return w.rearrange("(k p) c -> p k c", p=P)[:, k0:k0 + kn, c0:c0 + cn] if isinstance(c0, int) \
                else w.rearrange("(k p) c -> p k c", p=P)[:, k0:k0 + kn, bass.ds(c0, cn)]

        def up_units(st, u, w, width, col):
            for m in range(2):
                load(st, u + m, rows(w, 4 * m, 4, col, width), 4 * width)

        def down_units(st, u, w, j, half=False):
            n = 1 if half else 2
            for m in range(2):
                f0 = j * FT + m * n * P
                src = w[f0:f0 + n * P] if isinstance(f0, int) else w[bass.ds(f0, n * P)]
                load(st, u + m, src.rearrange("(k p) c -> p k c", p=P), n * D)

        sp.dma_start(x[:, :, :], io["x"][0].rearrange("(t p) d -> p t d", p=P)).then_inc(sem("x_in"), 16)
        sp.dma_start(g_row[:, :], io["mix_norm_g"][0].rearrange("(o d) -> o d", o=1).broadcast_to([P, D]))\
            .then_inc(sem("first_gain_in"), 16)
        sp.dma_start(mats[:, :, :], io["mats"]).then_inc(sem("mats_in"), 16)

        with sp.Fori(0, DEPTH) as l:
            st = Stream(l * (LAYER_UNITS + DENSE_UNITS), l * ((LAYER_UNITS + DENSE_UNITS) // RAW))
            w_in, w_out = io["w_in"][l], io["w_out"][l]
            for c in range(IN_W // 512):
                up_units(st, 2 * c, w_in, 512, c * 512)
            for i, (c, k) in enumerate(((0, 0), (1, 0), (0, 4), (1, 4))):
                load(st, 10 + i, rows(w_out, k, 4, c * 512, 512))
            up_units(st, 14, io["wkv_x"][l], 512, 0)
            load(st, 16, rows(io["wkv_x"][l], 0, 4, 512, 512))
            up_units(st, 17, io["wq_x"][l], 512, 0)
            load(st, 19, rows(io["wkv_x"][l], 4, 4, 512, 512))
            for i in range(4):
                load(st, 20 + i, rows(io["wo_x"][l], 2 * (i % 2), 2, (i // 2) * 512, 512), 1024)
            with sp.If(l < 1):
                st = Stream(LAYER_UNITS, LAYER_UNITS // RAW)
                w13, w2 = io["w13_dense"][0], io["w2_dense"][0]
                up_units(st, 0, w13, FT, FD)
                up_units(st, 2, w13, FT, 0)
                with sp.Fori(1, DENSE_STEPS) as j:
                    sj = Stream(LAYER_UNITS + (j - 1) * 6, LAYER_UNITS // RAW + (j - 1))
                    up_units(sj, 4, w13, FT, FD + j * FT)
                    up_units(sj, 6, w13, FT, j * FT)
                    down_units(sj, 8, w2, j - 1)
                e = 4 + 6 * (DENSE_STEPS - 1)
                up_units(st, e, w13, FT // 2, FD + DENSE_STEPS * FT)
                up_units(st, e + 2, w13, FT // 2, DENSE_STEPS * FT)
                down_units(st, e + 4, w2, DENSE_STEPS - 1)
                down_units(st, e + 6, w2, DENSE_STEPS, half=True)

        def item(i, w13, w2):
            st = Stream(i * ITEM_UNITS + MOE_BASE, i * (ITEM_UNITS // RAW) + MOE_BASE // RAW)
            up_units(st, 0, w13, FT, FE)
            up_units(st, 2, w13, FT, 0)
            with sp.Fori(1, ITEM_STEPS) as j:
                sj = Stream(i * ITEM_UNITS + (j - 1) * 6 + MOE_BASE,
                            i * (ITEM_UNITS // RAW) + (j - 1) + MOE_BASE // RAW)
                up_units(sj, 4, w13, FT, j * FT + FE)
                up_units(sj, 6, w13, FT, j * FT)
                down_units(sj, 8, w2, j - 1)
            down_units(st, 4 + 6 * (ITEM_STEPS - 1), w2, ITEM_STEPS - 1)

        with sp.Fori(0, NE) as i:
            item(i, io["w13_moe"][0, i], io["w2_moe"][0, i])
        sp.wait_ge(sem("info_ready"), 1)
        n_items = sp.value_load(info[0:1, 0:1], min_val=NE, max_val=ITEMS)
        with sp.Fori(NE, ITEMS) as i:
            with sp.If(n_items > i):
                e = sp.value_load(info[0:1, bass.ds(i - (NE - 1), 1)], min_val=0, max_val=NE - 1)
                item(i, io["w13_moe"][0, e], io["w2_moe"][0, e])
            sp.nop()
        for t in range(NT):
            sp.wait_ge(sem("xn_ready"), 2 * (3 * DEPTH + 1) + t + 1)
            sp.dma_start(io["out"][0, t * P:(t + 1) * P, :], xn[:, t, :]).then_inc(sem("out_done"), 16)
        sp.wait_ge(sem("out_done"), 16 * NT)

    @block.gpsimd
    def _(pool):
        def load_gain(m, row):
            pool.wait_ge(sem("xn_ready"), m * 2)
            pool.dma_start(g_row[:, :], row.rearrange("(o d) -> o d", o=1).broadcast_to([P, D]))\
                .then_inc(sem("gain_in"), 16)

        pool.memset(rel[:, :], 1.0).then_inc(sem("rel_ones"), 1)
        pool.wait_ge(sem("rel_ones"), 1)
        pool.dma_start(rel[0:BUCKETS, :], io["rel_bias"]).then_inc(sem("table_in"), 16)
        pool.dma_start(table, io["bias_table"]).then_inc(sem("table_in"), 16)
        pool.wait_ge(sem("x_in"), 16)
        pool.dma_start(mem_sb, io["mem"][0].rearrange("(t p) d -> p t d", p=P)).then_inc(sem("mem_in"), 16)
        load_gain(1, io["mem_norm_g"])
        pool.dma_start(pool_inv[:, :, :], io["pool_inv"]).then_inc(sem("params_in"), 16)
        pool.wait_ge(sem("skew_rows"), 1)
        pool.dma_start(skew.ap(), skew_rows.unsqueeze(1).broadcast_to([HEADS, P, SKEW_W])).then_inc(sem("skew_out"), 16)
        for l in range(DEPTH):
            if l:
                pool.wait_ge(sem("x_ready"), l * 3 + 1)
            pool.dma_start(conv_w[:, :, :], io["conv_w"][l].rearrange("k (b p) -> p k b", p=P), allow_slow_non_contiguous=True)\
                .then_inc(sem("params_in"), 16)
            pool.dma_start(pool_w[:, :, :], io["pool_w"][l].rearrange("(b h) c d -> (h c) b d", h=2))\
                .then_inc(sem("params_in"), 16)
            pool.dma_start(pool_s[:, :], io["pool_scale"][l].rearrange("(b p) -> p b", p=P), allow_slow_non_contiguous=True)\
                .then_inc(sem("params_in"), 16)
            load_gain(l * 3 + 2, io["xattn_norm_g"][l])
            if l == 0:
                pool.wait_ge(sem("skew_out"), 16)
                pool.dma_start(bias[:, :, :], bass.AP(skew, P - 1, [[SKEW_W - 1, P], [P * SKEW_W, HEADS], [1, T]]))\
                    .then_inc(sem("bias_in"), 16)
                pool.dma_start(router[:, :, :], io["router_w"][0].rearrange("(k p) e -> p k e", p=P))\
                    .then_inc(sem("router_in"), 16)
                pool.dma_start(less8[:, :, :], io["less8"]).then_inc(sem("router_in"), 16)
            load_gain(l * 3 + 3, io["ffn_norm_g"][l])
            load_gain(l * 3 + 4, io["mix_norm_g"][l + 1] if l + 1 < DEPTH else io["final_norm_g"])

    @block.scalar
    def _(act):
        def hi(st, u, width=UNIT):
            act.wait_ge(sem(f"raw{u % RAW}"), st.landed(u))
            n = width // 2
            for half in range(2):
                act.wait_ge(sem("unit_used"), st.upto(u, half))
                act.activation(w_hi[:, u % SPLIT, half, 0:n], raw[:, u % RAW, half * n:(half + 1) * n], ACT.Copy)\
                    .then_inc(sem("unit_hi"), 1)

        def norm(m, src):
            act.activation(xn[:, 1, :], src[:, 1, :], ACT.Square, accum_out=ss[:, 1:2])\
                .then_inc(sem("square_act"), 1)
            act.wait_ge(sem("square_act"), m + 1)
            act.wait_ge(sem("square_dve"), m + 1)
            act.activation(lnv[:, :], ss[:, :], ACT.Ln, scale=1.0 / D, bias=eps_col[:, 0:1])\
                .then_inc(sem("ln_act"), 1)
            act.wait_ge(sem("ln_act"), m + 1)
            act.activation(r0[:, :], lnv[:, :], ACT.Exp, scale=-0.5).then_inc(sem("rstd_guess"), 1)

        def turned_hi(m, banks, dst):
            for i in range(4):
                t, half = i // 2, i % 2
                act.wait_ge(sem("xT_mm"), m * 4 + i + 1)
                act.activation(dst[:, 4 * half:4 * half + 4, t * P:(t + 1) * P], banks4(banks[i]), ACT.Copy)\
                    .then_inc(sem("xT_hi"), 1)

        def silu_tiles(width, tiles, g_bank):
            for t in range(tiles):
                act.activation(hid[:, t, 0:width], bank[g_bank + t][:, 0:width], ACT.Silu)\
                    .then_inc(sem("silu"), 1)

        def hidT_hi(width, tiles, g_bank):
            for t in range(tiles):
                n = width // P
                act.activation(yT_hi[:, 0:n, t * P:(t + 1) * P], banks4(g_bank + t)[:, 0:n, :], ACT.Copy)\
                    .then_inc(sem("hidT_hi"), 1)

        act.wait_ge(sem("consts"), 1)
        act.preload_act_table_set("natural_log_exp_and_others")
        act.wait_ge(sem("x_in"), 16)
        norm(0, x)
        turned_hi(0, (0, 1, 2, 3), xT_hi)

        with act.Fori(0, DEPTH) as l:
            l1 = l + 1
            st = Stream(l * (LAYER_UNITS + DENSE_UNITS), l * ((LAYER_UNITS + DENSE_UNITS) // RAW))
            for u in range(4):
                hi(st, u)
            used(act, st, 1)
            for b in range(2):
                act.activation(qk[:, 0, 2 * b:2 * b + 2, :], bank[4 + b][:, :].rearrange("p (c t) -> p c t", c=2),
                               ACT.Copy, scale=DH ** -0.5).then_inc(sem("q_sb"), 1)
            hi(st, 4)
            with act.If(l < 1):
                act.preload_act_table_set("natural_log_exp_and_others")
                act.wait_ge(sem("mem_in"), 16)
                norm(1, mem_sb)
            hi(st, 5)
            hi(st, 6)
            with act.If(l < 1):
                turned_hi(1, (4, 5, 6, 7), memT_hi)
            hi(st, 7)
            used(act, st, 5)
            for t in range(NT):
                act.activation(v[:, t, :], bank[t][:, :], ACT.Copy).then_inc(sem("v_sb"), 1)
            for h in range(HEADS):
                act.wait_ge(sem("logits"), l * HEADS + h + 1)
                for t, (a, b) in enumerate(((0, P), (P, 3 * P))):
                    act.activation(prob[:, h % 2, a:b], prob[:, h % 2, a:b], ACT.Exp, bias=nmx[:, h % 2, t:t + 1],
                                   accum_out=den[:, t, h:h + 1]).then_inc(sem("exp"), 1)
                if h in (1, 4, 6):
                    hi(st, {1: 8, 4: 9, 6: 10}[h])
            hi(st, 11)
            for t in range(NT):
                act.wait_ge(sem("yTok_mm"), l * 2 + t + 1)
                act.activation(yT_hi[:, 0:4, t * P:(t + 1) * P], banks4(4 + t), ACT.Copy).then_inc(sem("yT_hi"), 1)
            act.wait_ge(sem("pool_mm"), l1)
            act.wait_ge(sem("params_in"), l * 48 + 64)
            for b in range(2):
                act.activation(yT_hi[:, 4 + b, :], bank[2][:, b * T:(b + 1) * T], ACT.Copy, scale=pool_s[:, b:b + 1])\
                    .then_inc(sem("yT_hi"), 1)
            used(act, st, 9)
            act.activation(conv_c, bank[6][:, :].rearrange("p (b t) -> p b t", b=2), ACT.Copy)\
                .then_inc(sem("c_sb"), 1)
            hi(st, 12)
            act.wait_ge(sem("conv_y"), l1)
            act.activation(yT_hi[:, 6:8, :], conv_y, ACT.Copy).then_inc(sem("yT_hi"), 1)
            for u in range(13, 16):
                hi(st, u)
            act.wait_ge(sem("x_ready"), l * 3 + 2)
            norm(l * 3 + 2, x)
            hi(st, 16)
            turned_hi(l * 3 + 2, (0, 1, 2, 3), xT_hi)
            used(act, st, 15)
            for b in range(2):
                act.activation(qk[:, 1, 2 * b:2 * b + 2, :], bank[6 + b][:, :].rearrange("p (c t) -> p c t", c=2),
                               ACT.Copy).then_inc(sem("xk_sb"), 1)
            for u in range(17, 20):
                hi(st, u)
            used(act, st, 18)
            for b in range(2):
                act.activation(qk[:, 0, 2 * b:2 * b + 2, :], bank[b][:, :].rearrange("p (c t) -> p c t", c=2),
                               ACT.Copy).then_inc(sem("xq_sb"), 1)
            hi(st, 20, 1024)
            hi(st, 21, 1024)
            used(act, st, 19)
            for t in range(NT):
                act.activation(v[:, t, :], bank[4 + t][:, :], ACT.Copy).then_inc(sem("xv_sb"), 1)
            for h in range(XHEADS):
                act.wait_ge(sem("xmax"), l * XHEADS + h + 1)
                if h >= 2:
                    act.wait_ge(sem("xprobT_mm"), l * XHEADS + h - 1)
                for t in range(NT):
                    act.activation(prob[:, h % 2, t * T:(t + 1) * T], bank[2 + h % 2][:, t * T:(t + 1) * T], ACT.Exp,
                                   scale=XSCALE, bias=nmx[:, h % 2, t:t + 1],
                                   accum_out=den[:, t, h:h + 1]).then_inc(sem("xexp"), 1)
            hi(st, 22, 1024)
            for t in range(NT):
                act.wait_ge(sem("xyT_mm"), l * 2 + t + 1)
                act.activation(yT_hi[:, 0:4, t * P:(t + 1) * P], banks4(4 + t), ACT.Copy).then_inc(sem("xyT_hi"), 1)
            hi(st, 23, 1024)
            act.preload_act_table_set("natural_log_exp_and_others")
            act.wait_ge(sem("x_ready"), l * 3 + 3)
            norm(l * 3 + 3, x)
            turned_hi(l * 3 + 3, (4, 5, 6, 7), xT_hi)
            with act.If(l < 1):
                st = Stream(LAYER_UNITS, LAYER_UNITS // RAW)
                act.preload_act_table(ACT.Silu)
                for u in range(4):
                    hi(st, u)
                used(act, st, 3)
                silu_tiles(FT, NT, 2)
                with act.Fori(1, DENSE_STEPS) as j:
                    sj = Stream(LAYER_UNITS + (j - 1) * 6, LAYER_UNITS // RAW + (j - 1))
                    hi(sj, 4)
                    hi(sj, 5)
                    act.wait_ge(sem("hidT_mm"), j)
                    hidT_hi(FT, NT, 2)
                    for u in range(6, 10):
                        hi(sj, u)
                    used(act, sj, 7)
                    silu_tiles(FT, NT, 2)
                e = 4 + 6 * (DENSE_STEPS - 1)
                hi(st, e, 1024)
                hi(st, e + 1, 1024)
                act.wait_ge(sem("hidT_mm"), DENSE_STEPS)
                hidT_hi(FT, NT, 2)
                hi(st, e + 2, 1024)
                hi(st, e + 3, 1024)
                hi(st, e + 4)
                hi(st, e + 5)
                used(act, st, e + 3)
                silu_tiles(FT // 2, NT, 2)
                hi(st, e + 6, 1024)
                act.wait_ge(sem("hidT_mm"), DENSE_STEPS + 1)
                hidT_hi(FT // 2, NT, 2)
                hi(st, e + 7, 1024)
                act.preload_act_table_set("natural_log_exp_and_others")
                act.wait_ge(sem("x_ready"), 4)
                norm(4, x)
                turned_hi(4, (0, 1, 2, 3), xT_hi)
            act.nop()

        act.wait_ge(sem("router_in"), 32)
        act.activation(router_parts[:, :, 0:NE], router[:, :, :], ACT.Copy).then_inc(sem("router_hi"), 1)
        act.wait_ge(sem("top_diff"), 1)
        act.activation(top[:, 2, :], top[:, 1, :], ACT.Exp).then_inc(sem("top_exp"), 1)
        act.preload_act_table(ACT.Silu)

        def gathered_hi(i):
            for b in range(2):
                act.wait_ge(sem("gather_mm"), i * 2 + b + 1)
                act.activation(xgT_hi[:, 4 * b:4 * b + 4, :], banks4(6 + b), ACT.Copy).then_inc(sem("gather_hi"), 1)

        def rows_out(i):
            act.wait_ge(sem("unit_used"), i * (2 * ITEM_UNITS) + 2 * (MOE_BASE + SPLIT))
            for col in range(2):
                act.activation(y_sb[:, col * 512:(col + 1) * 512], bank[4 + col][:, :], ACT.Copy)\
                    .then_inc(sem("rows_sb"), 1)

        act.sem_inc(sem("rows_sb"), 2)
        gathered_hi(0)
        act.wait_ge(sem("info_ready"), 1)
        n_items = act.value_load(info[0:1, 0:1], min_val=NE, max_val=ITEMS)
        with act.Fori(0, ITEMS) as i:
            with act.If(n_items > i):
                st = Stream(i * ITEM_UNITS + MOE_BASE, i * (ITEM_UNITS // RAW) + MOE_BASE // RAW)
                hi(st, 0)
                hi(st, 1)
                with act.If(i > 0):
                    rows_out(i)
                for u in range(2, 6):
                    hi(st, u)
                used(act, st, 3)
                silu_tiles(FT, 1, 2)
                with act.Fori(1, ITEM_STEPS) as j:
                    sj = Stream(i * ITEM_UNITS + (j - 1) * 6 + MOE_BASE,
                                i * (ITEM_UNITS // RAW) + (j - 1) + MOE_BASE // RAW)
                    act.wait_ge(sem("hidT_mm"), i * ITEM_STEPS + j + DENSE_TURNS)
                    hidT_hi(FT, 1, 2)
                    for u in range(6, 10):
                        hi(sj, u)
                    used(act, sj, 7)
                    silu_tiles(FT, 1, 2)
                    hi(sj, 10)
                    hi(sj, 11)
                act.wait_ge(sem("hidT_mm"), i * ITEM_STEPS + ITEM_STEPS + DENSE_TURNS)
                hidT_hi(FT, 1, 2)
                gathered_hi(i + 1)
            act.nop()
        rows_out(n_items)
        act.preload_act_table_set("natural_log_exp_and_others")
        act.wait_ge(sem("x_final"), 1)
        norm(3 * DEPTH + 1, x)

    @block.vector
    def _(dve):
        c = Chain(dve, sem("dve_step"))

        def lo(st, u, width=UNIT):
            n = width // 2
            for half in range(2):
                dve.wait_ge(sem("unit_hi"), st.upto(u, half))
                dve.tensor_tensor(w_lo[:, u % SPLIT, half, 0:n], raw[:, u % RAW, half * n:(half + 1) * n],
                                  w_hi[:, u % SPLIT, half, 0:n].bitcast(F32), ALU.subtract)\
                    .then_inc(sem("raw_free"), 1)

        def rest(out, src, hi_part):
            return dve.tensor_tensor(out, src, hi_part.bitcast(F32), ALU.subtract)

        def norm(m, src):
            dve.tensor_tensor_reduce(xn[:, 0, :], src[:, 0, :], src[:, 0, :], 1.0, 0.0, ALU.mult, ALU.add,
                                     ss[:, 0:1]).then_inc(sem("square_dve"), 1)
            dve.wait_ge(sem("square_dve"), m + 1)
            dve.wait_ge(sem("square_act"), m + 1)
            dve.tensor_scalar(nw[:, 0, :], ss[:, :], 1.0 / D, EPS, ALU.mult, ALU.add).then_inc(sem("newton"), 1)
            dve.wait_ge(sem("rstd_guess"), m + 1)
            dve.tensor_tensor(nw[:, 1, :], r0[:, :], r0[:, :], ALU.mult).then_inc(sem("newton"), 1)
            dve.wait_ge(sem("newton"), m * 5 + 2)
            dve.tensor_tensor(nw[:, 2, :], nw[:, 0, :], nw[:, 1, :], ALU.mult).then_inc(sem("newton"), 1)
            dve.wait_ge(sem("newton"), m * 5 + 3)
            dve.tensor_scalar(nw[:, 1, :], nw[:, 2, :], -0.5, 1.5, ALU.mult, ALU.add).then_inc(sem("newton"), 1)
            dve.wait_ge(sem("newton"), m * 5 + 4)
            dve.tensor_tensor(rstd[:, :], r0[:, :], nw[:, 1, :], ALU.mult).then_inc(sem("newton"), 1)
            dve.wait_ge(sem("newton"), m * 5 + 5)
            if isinstance(m, int) and m == 0:
                dve.wait_ge(sem("first_gain_in"), 16)
            else:
                dve.wait_ge(sem("gain_in"), m * 16)
            for t in range(NT):
                dve.scalar_tensor_tensor(xn[:, t, :], src[:, t, :], rstd[:, t:t + 1], g_row[:, :],
                                         ALU.mult, ALU.mult).then_inc(sem("xn_ready"), 1)

        def turned_lo(m, banks, dst_hi, dst_lo):
            for i in range(4):
                t, half = i // 2, i % 2
                dve.wait_ge(sem("xT_hi"), m * 4 + i + 1)
                s = (slice(None), slice(4 * half, 4 * half + 4), slice(t * P, (t + 1) * P))
                rest(dst_lo[s], banks4(banks[i]), dst_hi[s]).then_inc(sem("xT_lo"), 1)

        def add_to_x(st, units, banks):
            for col in range(2):
                used(dve, st, units[col])
                for t in range(NT):
                    s = slice(col * 512, (col + 1) * 512)
                    last = dve.tensor_tensor(x[:, t, s], x[:, t, s], bank[banks[2 * col + t]][:, :], ALU.add)
            last.then_inc(sem("x_ready"), 1)

        def gate_tiles(width, tiles, silus):
            for t in range(tiles):
                dve.wait_ge(sem("silu"), silus + (t + 1))
                dve.tensor_tensor(hid[:, t, 0:width], hid[:, t, 0:width], bank[t][:, 0:width], ALU.mult)\
                    .then_inc(sem("hid_ready"), 1)

        def hidT_lo(width, tiles, g_bank, his):
            n = width // P
            for t in range(tiles):
                dve.wait_ge(sem("hidT_hi"), his + (t + 1))
                s = (slice(None), slice(0, n), slice(t * P, (t + 1) * P))
                rest(yT_lo[s], banks4(g_bank + t)[:, 0:n, :], yT_hi[s]).then_inc(sem("hidT_lo"), 1)

        dve.sem_inc(sem("raw_free"), 2 * RAW)
        dve.memset(eps_col[:, :], EPS).then_inc(sem("consts"), 1)
        dve.memset(zeros[:, :], 0.0).then_inc(sem("zeros"), 1)
        c.step(dve.memset(conv_u[:, :, :], 0.0))
        c.step(dve.memset(pool_a[:, :, :], 0.0))
        c.step(dve.memset(pool_b[:, :, :], 0.0))
        c.link(dve.memset(places[:, :, :, :], -1.0))
        dve.wait_ge(sem("x_in"), 16)
        norm(0, x)
        turned_lo(0, (0, 1, 2, 3), xT_hi, xT_lo)
        dve.wait_ge(sem("skew_mm"), 1)
        dve.tensor_copy(skew_rows, bank[7][0:HEADS, 0:SKEW_W]).then_inc(sem("skew_rows"), 1)
        dve.sem_inc(sem("x_ready"), 1)
        head = c.n

        with dve.Fori(0, DEPTH) as l:
            l1 = l + 1
            c.restart(l * DVE_LAYER + head)
            st = Stream(l * (LAYER_UNITS + DENSE_UNITS), l * ((LAYER_UNITS + DENSE_UNITS) // RAW))
            for u in range(5):
                lo(st, u)
            used(dve, st, 3)
            for b in range(2):
                dve.tensor_copy(qk[:, 1, 2 * b:2 * b + 2, :], bank[6 + b][:, :].rearrange("p (c t) -> p c t", c=2))\
                    .then_inc(sem("k_sb"), 1)
            with dve.If(l < 1):
                dve.wait_ge(sem("mem_in"), 16)
                norm(1, mem_sb)
            lo(st, 5)
            lo(st, 6)
            with dve.If(l < 1):
                turned_lo(1, (4, 5, 6, 7), memT_hi, memT_lo)
            lo(st, 7)
            A, B = pool_a[:, :, 16:], pool_b[:, :, 16:]
            u_pool = bank[2][:, :].rearrange("p (b t) -> p b t", b=2)

            def back(buf, k):
                return buf[:, :, 16 - k:16 - k + T]

            dve.wait_ge(sem("bias_in"), 16)
            for i in range(HEADS + 1):
                if i < HEADS:
                    h = i
                    hold(dve, "logits_mm", l * HEADS + h + 1)
                    if h >= 2:
                        hold(dve, "probT_mm", l * HEADS + h - 1)
                    for t, (a, b, s0) in enumerate(((0, P, P), (P, 3 * P, 0))):
                        c.step(dve.tensor_tensor_reduce(prob[:, h % 2, a:b], bank[6 + h % 2][:, a:b],
                                                        bias[:, h, s0:T], 1.0, 3.0 * MASKED, ALU.add, ALU.max,
                                                        mx[:, h % 2, t:t + 1]))
                    c.wait()
                    dve.tensor_scalar(nmx[:, h % 2, :], mx[:, h % 2, :], -1.0, None, ALU.mult)\
                        .then_inc(sem("logits"), 1)
                if i >= 1:
                    h = i - 1
                    dve.wait_ge(sem("probT_mm"), l * HEADS + h + 1)
                    if h >= 2:
                        dve.wait_ge(sem("pv_mm"), l * HEADS + h - 1)
                    dve.tensor_copy(probT[:, h % 2, 0:3 * P], bank[h % 2][:, 0:3 * P]).then_inc(sem("probT_sb"), 1)
                if i == 2:
                    lo(st, 8)
                elif i == 5:
                    lo(st, 9)
                elif i == 6:
                    used(dve, st, 7)
                    c.link(dve.tensor_copy(A, u_pool))
                    c.link(dve.tensor_tensor(B, A, back(pool_a, 1), ALU.add))
                    c.step(dve.tensor_tensor(A[64:128, 0, :], B[64:128, 0, :], back(pool_b, 2)[64:128, 0, :], ALU.add))
                    c.link(dve.tensor_tensor(A[:, 1, :], B[:, 1, :], back(pool_b, 2)[:, 1, :], ALU.add))
                elif i == 7:
                    c.link(dve.tensor_tensor(B[:, 1, :], A[:, 1, :], back(pool_a, 4)[:, 1, :], ALU.add))
                    c.link(dve.tensor_tensor(A[64:128, 1, :], B[64:128, 1, :], back(pool_b, 8)[64:128, 1, :], ALU.add))
                    dve.wait_ge(sem("params_in"), l * 48 + 64)
                    c.step(dve.tensor_tensor(pooled[0:64], B[0:64], pool_inv[0:64, :, :], ALU.mult))
                    c.link(dve.tensor_tensor(pooled[64:128], A[64:128], pool_inv[64:128, :, :], ALU.mult))
                    dve.tensor_tensor(pooled, pooled, u_pool, ALU.subtract).then_inc(sem("pooled"), 1)
                elif i == HEADS:
                    lo(st, 10)
            dve.wait_ge(sem("exp"), l1 * (2 * HEADS))
            c.link(dve.reciprocal(rden[:, :, :], den[:, :, :]))
            dve.wait_ge(sem("pv_mm"), l1 * HEADS)
            for t in range(NT):
                dve.tensor_tensor(y_tok[:, t, :].rearrange("p (h d) -> p h d", h=HEADS),
                                  bank[4 + t][:, :].rearrange("p (h d) -> p h d", h=HEADS),
                                  rden[:, t, :].unsqueeze(2).broadcast_to([P, HEADS, DH]), ALU.mult)\
                    .then_inc(sem("y_tok"), 1)
            lo(st, 11)
            for t in range(NT):
                dve.wait_ge(sem("yT_hi"), l * 5 + 1 + t)
                s = (slice(None), slice(0, 4), slice(t * P, (t + 1) * P))
                rest(yT_lo[s], banks4(4 + t), yT_hi[s]).then_inc(sem("yT_lo"), 1)
            for b in range(2):
                dve.wait_ge(sem("yT_hi"), l * 5 + 4)
                dve.scalar_tensor_tensor(yT_lo[:, 4 + b, :], bank[2][:, b * T:(b + 1) * T], pool_s[:, b:b + 1],
                                         yT_hi[:, 4 + b, :].bitcast(F32), ALU.mult, ALU.subtract)\
                    .then_inc(sem("yT_lo"), 1)
            dve.wait_ge(sem("c_sb"), l1)
            now_u, h_bank, b_bank = conv_u[:, :, 2:], bank[7], bank[3]
            c.link(dve.tensor_tensor(now_u, conv_c, h_bank[:, :].rearrange("p (b t) -> p b t", b=2), ALU.mult))
            for b in range(2):
                c.step(dve.tensor_scalar(conv_y[:, b, :], now_u[:, b, :], conv_w[:, 0, b:b + 1], None, ALU.mult))
            c.wait()
            for tap in (1, 2):
                for b in range(2):
                    c.step(dve.scalar_tensor_tensor(conv_y[:, b, :], conv_u[:, b, 2 - tap:2 - tap + T],
                                                    conv_w[:, tap, b:b + 1], conv_y[:, b, :], ALU.mult, ALU.add))
                c.wait()
            dve.tensor_tensor(conv_y, conv_y, b_bank[:, :].rearrange("p (b t) -> p b t", b=2), ALU.mult)\
                .then_inc(sem("conv_y"), 1)
            lo(st, 12)
            dve.wait_ge(sem("yT_hi"), l * 5 + 5)
            dve.wait_ge(sem("conv_y"), l1)
            rest(yT_lo[:, 6:8, :], conv_y, yT_hi[:, 6:8, :]).then_inc(sem("yT_lo"), 1)
            lo(st, 13)
            lo(st, 14)
            lo(st, 15)
            add_to_x(st, (12, 13), (0, 1, 4, 5))
            dve.wait_ge(sem("x_ready"), l * 3 + 2)
            norm(l * 3 + 2, x)
            lo(st, 16)
            turned_lo(l * 3 + 2, (0, 1, 2, 3), xT_hi, xT_lo)
            for u in range(17, 20):
                lo(st, u)
            lo(st, 20, 1024)
            lo(st, 21, 1024)
            for i in range(XHEADS + 1):
                if i < XHEADS:
                    h = i
                    dve.wait_ge(sem("xlogits_mm"), l * XHEADS + h + 1)
                    if h >= 2:
                        dve.wait_ge(sem("xexp"), (l * XHEADS + h - 1) * NT)
                    c.link(dve.tensor_reduce(mx[:, h % 2, :], bank[2 + h % 2][:, :].rearrange("p (t m) -> p t m", t=NT),
                                             AX.X, ALU.max))
                    dve.tensor_scalar(nmx[:, h % 2, :], mx[:, h % 2, :], -XSCALE, None, ALU.mult)\
                        .then_inc(sem("xmax"), 1)
                if i >= 1:
                    h = i - 1
                    dve.wait_ge(sem("xprobT_mm"), l * XHEADS + h + 1)
                    if h >= 2:
                        dve.wait_ge(sem("xpv_mm"), l * XHEADS + h - 1)
                    dve.tensor_copy(probT[:, h % 2, :], bank[h % 2][:, :]).then_inc(sem("xprobT_sb"), 1)
            dve.wait_ge(sem("xexp"), l1 * (NT * XHEADS))
            c.link(dve.reciprocal(rden[:, :, 0:XHEADS], den[:, :, 0:XHEADS]))
            dve.wait_ge(sem("xpv_mm"), l1 * XHEADS)
            for t in range(NT):
                dve.tensor_tensor(y_tok[:, t, :].rearrange("p (h d) -> p h d", h=XHEADS),
                                  bank[6 + t][:, :].rearrange("p (h d) -> p h d", h=XHEADS),
                                  rden[:, t, 0:XHEADS].unsqueeze(2).broadcast_to([P, XHEADS, XDH]), ALU.mult)\
                    .then_inc(sem("xy_tok"), 1)
            lo(st, 22, 1024)
            for t in range(NT):
                dve.wait_ge(sem("xyT_hi"), l * 2 + t + 1)
                s = (slice(None), slice(0, 4), slice(t * P, (t + 1) * P))
                rest(yT_lo[s], banks4(4 + t), yT_hi[s]).then_inc(sem("xyT_lo"), 1)
            lo(st, 23, 1024)
            add_to_x(st, (21, 23), (0, 1, 2, 3))
            dve.wait_ge(sem("x_ready"), l * 3 + 3)
            norm(l * 3 + 3, x)
            turned_lo(l * 3 + 3, (4, 5, 6, 7), xT_hi, xT_lo)
            with dve.If(l < 1):
                st = Stream(LAYER_UNITS, LAYER_UNITS // RAW)
                for u in range(4):
                    lo(st, u)
                gate_tiles(FT, NT, 0)
                with dve.Fori(1, DENSE_STEPS) as j:
                    sj = Stream(LAYER_UNITS + (j - 1) * 6, LAYER_UNITS // RAW + (j - 1))
                    lo(sj, 4)
                    lo(sj, 5)
                    hidT_lo(FT, NT, 2, (j - 1) * NT)
                    for u in range(6, 10):
                        lo(sj, u)
                    gate_tiles(FT, NT, j * NT)
                e = 4 + 6 * (DENSE_STEPS - 1)
                lo(st, e, 1024)
                lo(st, e + 1, 1024)
                hidT_lo(FT, NT, 2, (DENSE_STEPS - 1) * NT)
                lo(st, e + 2, 1024)
                lo(st, e + 3, 1024)
                lo(st, e + 4)
                lo(st, e + 5)
                gate_tiles(FT // 2, NT, DENSE_STEPS * NT)
                lo(st, e + 6, 1024)
                hidT_lo(FT // 2, NT, 2, DENSE_STEPS * NT)
                lo(st, e + 7, 1024)
                add_to_x(st, (e + 7, e + 7), (4, 5, 6, 7))
                dve.wait_ge(sem("x_ready"), 4)
                norm(4, x)
                turned_lo(4, (0, 1, 2, 3), xT_hi, xT_lo)
            dve.nop()
        assert c.n == DVE_LAYER, c.n
        c.restart(head + DEPTH * DVE_LAYER)

        dve.wait_ge(sem("router_in"), 32)
        dve.wait_ge(sem("router_hi"), 1)
        rest(router_parts[:, :, NE:2 * NE], router[:, :, :], router_parts[:, :, 0:NE]).then_inc(sem("router_lo"), 1)
        dve.wait_ge(sem("router_mm"), 1)

        def over_experts(ap):
            return ap.unsqueeze(2).broadcast_to([P, NT, NE])

        dve.tensor_copy(parts_sb, bank[0][0:2 * NE, 0:T]).then_inc(sem("parts_sb"), 1)
        dve.wait_ge(sem("parts_mm"), 1)
        parts = bank[2][:, 0:NT * 2 * NE].rearrange("p (t a e) -> p t a e", t=NT, a=2)
        c.link(dve.tensor_copy(lg_lo[:, :, :], parts[:, :, 1, :]))
        c.link(dve.tensor_tensor(lg[:, :, :], lg_lo[:, :, :], parts[:, :, 0, :], ALU.add))

        def pick_first(best, place, out):
            c.link(dve.tensor_reduce(best, lg[:, :, :], AX.X, ALU.max))
            c.link(dve.tensor_tensor(tmp8[:, :, :], lg[:, :, :], over_experts(best), ALU.is_equal))
            c.link(dve.tensor_tensor(tmp8[:, :, :], tmp8[:, :, :], less8[:, :, :], ALU.mult))
            c.link(dve.tensor_reduce(place, tmp8[:, :, :], AX.X, ALU.min))
            c.link(dve.tensor_tensor(out, less8[:, :, :], over_experts(place), ALU.is_equal))

        pick_first(top[:, 0, :], top[:, 3, :], sel1[:, :, :])
        c.link(dve.scalar_tensor_tensor(lg[:, :, :], sel1[:, :, :], -3e38, lg[:, :, :], ALU.mult, ALU.add))
        pick_first(top[:, 4, :], top[:, 5, :], sel2[:, :, :])
        dve.tensor_tensor(top[:, 1, :], top[:, 4, :], top[:, 0, :], ALU.subtract).then_inc(sem("top_diff"), 1)
        dve.tensor_tensor(mask[:, :, :], sel1[:, :, :], sel2[:, :, :], ALU.add).then_inc(sem("mask"), 1)
        dve.wait_ge(sem("top_exp"), 1)
        c.link(dve.tensor_scalar(top[:, 6, :], top[:, 2, :], 1.0, None, ALU.add))
        c.link(dve.reciprocal(top[:, 7, :], top[:, 6, :]))
        c.link(dve.tensor_tensor(top[:, 6, :], top[:, 2, :], top[:, 7, :], ALU.mult))
        c.step(dve.tensor_tensor(sel1[:, :, :], sel1[:, :, :], over_experts(top[:, 7, :]), ALU.mult))
        c.link(dve.tensor_tensor(sel2[:, :, :], sel2[:, :, :], over_experts(top[:, 6, :]), ALU.mult))
        c.link(dve.tensor_tensor(gates[:, :, :], sel1[:, :, :], sel2[:, :, :], ALU.add))
        dve.wait_ge(sem("rank_mm"), 1)
        dve.wait_ge(sem("mask"), 1)
        rank = bank[1][:, 0:NT * NE].rearrange("p (t e) -> p t e", t=NT)
        c.link(dve.scalar_tensor_tensor(tmp8[:, :, :], rank, 1.0, mask[:, :, :], ALU.add, ALU.mult))
        c.link(dve.tensor_scalar(tmp8[:, :, :], tmp8[:, :, :], -1.0, None, ALU.add))
        c.step(dve.tensor_copy(places[:, 0:NE, 0, :].rearrange("p e t -> p t e"), tmp8[:, :, :]))
        c.step(dve.tensor_copy(places[:, 0:NE, 1, :].rearrange("p e t -> p t e"), gates[:, :, :]))
        def select(out, places_of, with_gate):
            for t in range(NT):
                if with_gate:
                    last = dve.tensor_scalar(out[:, t, :], iota, places_of[:, 0, t:t + 1], places_of[:, 1, t:t + 1],
                                             ALU.is_equal, ALU.mult)
                else:
                    last = dve.tensor_scalar(out[:, t, :], iota, places_of[:, 0, t:t + 1], None, ALU.is_equal)
            return last

        c.wait()
        select(S, places[:, 0, :, :], False).then_inc(sem("select"), 1)
        c.link(dve.tensor_scalar(over[:, :], bank[1][:, 2 * NE:3 * NE], float(P), None, ALU.is_gt))
        c.link(dve.tensor_reduce(first[:, 0:1], over[:, :], AX.X, ALU.add))
        c.link(dve.tensor_scalar(first[:, 0:1], first[:, 0:1], float(NE), None, ALU.add))
        c.link(dve.tensor_scalar(lg[:, :, :], tmp8[:, :, :], -float(P - 1), None, ALU.add))
        for k in range(OVER):
            c.link(dve.tensor_tensor(pick[:, k, :], over[:, :], less8[:, 0, :], ALU.mult))
            c.link(dve.tensor_reduce(first[:, k + 1:k + 2], pick[:, k, :], AX.X, ALU.min))
            c.link(dve.tensor_scalar(pick[:, k, :], less8[:, 0, :], first[:, k + 1:k + 2], None, ALU.is_equal))
            c.link(dve.tensor_tensor(over[:, :], over[:, :], pick[:, k, :], ALU.subtract))
            picked = pick[:, k, :].unsqueeze(1).broadcast_to([P, NT, NE])
            c.link(dve.tensor_tensor(tmp8[:, :, :], lg[:, :, :], picked, ALU.mult))
            c.link(dve.tensor_reduce(top[:, 0, :], tmp8[:, :, :], AX.X, ALU.add))
            c.step(dve.tensor_scalar(places[:, NE + k, 0, :], top[:, 0, :], -1.0, None, ALU.add))
            c.link(dve.tensor_tensor(tmp8[:, :, :], gates[:, :, :], picked, ALU.mult))
            c.link(dve.tensor_reduce(places[:, NE + k, 1, :], tmp8[:, :, :], AX.X, ALU.add))
        c.link(dve.tensor_scalar(first[:, 1:OVER + 1], first[:, 1:OVER + 1], float(NE), float(NE - 1), ALU.add, ALU.min))
        dve.tensor_copy(info[0:1, :], first[0:1, :]).then_inc(sem("info_ready"), 1)
        dve.wait_ge(sem("info_ready"), 1)
        n_items = dve.value_load(info[0:1, 0:1], min_val=NE, max_val=ITEMS)

        def gathered_lo(i):
            for b in range(2):
                dve.wait_ge(sem("gather_hi"), i * 2 + b + 1)
                rest(xgT_lo[:, 4 * b:4 * b + 4, :], banks4(6 + b), xgT_hi[:, 4 * b:4 * b + 4, :])\
                    .then_inc(sem("gather_lo"), 1)

        def add_rows(i):
            for n in range(4):
                t, s = n // 2, slice(n % 2 * 512, (n % 2 + 1) * 512)
                dve.wait_ge(sem("scatter_mm"), i * 4 + n + 1)
                dve.tensor_tensor(x[:, t, s], x[:, t, s], bank[SCATTER[n]][:, :], ALU.add)\
                    .then_inc(sem("scatter_add"), 1)

        dve.sem_inc(sem("SgT"), 1)
        gathered_lo(0)
        routed = head + DEPTH * DVE_LAYER + c.n
        with dve.Fori(0, ITEMS) as i:
            with dve.If(n_items > i):
                c.restart(i * ITEM_CHAIN + routed)
                st = Stream(i * ITEM_UNITS + MOE_BASE, i * (ITEM_UNITS // RAW) + MOE_BASE // RAW)
                for u in range(5):
                    lo(st, u)
                gate_tiles(FT, 1, i * ITEM_STEPS + NT * DENSE_TURNS)
                with dve.If(i > 0):
                    add_rows(i)
                lo(st, 5)
                c.link(dve.tensor_copy(now[:, :, :, :], places[:, bass.ds(i, 2), :, :]))
                select(Sg, now[:, 0, :, :], True).then_inc(sem("select_gated"), 1)
                dve.wait_ge(sem("gather_mm"), i * 2 + 2)
                select(S, now[:, 1, :, :], False).then_inc(sem("select"), 1)
                with dve.Fori(1, ITEM_STEPS) as j:
                    sj = Stream(i * ITEM_UNITS + (j - 1) * 6 + MOE_BASE,
                                i * (ITEM_UNITS // RAW) + (j - 1) + MOE_BASE // RAW)
                    hidT_lo(FT, 1, 2, i * ITEM_STEPS + (j - 1) + NT * DENSE_TURNS)
                    for u in range(6, 10):
                        lo(sj, u)
                    gate_tiles(FT, 1, i * ITEM_STEPS + j + NT * DENSE_TURNS)
                    lo(sj, 10)
                    lo(sj, 11)
                hidT_lo(FT, 1, 2, i * ITEM_STEPS + (ITEM_STEPS - 1) + NT * DENSE_TURNS)
                dve.wait_ge(sem("select_mm"), i + 1)
                dve.tensor_copy(SgT[:, :, :], bank[1][:, 0:NT * P].rearrange("p (t r) -> p t r", t=NT))\
                    .then_inc(sem("SgT"), 1)
                gathered_lo(i + 1)
            dve.nop()
        add_rows(n_items)
        hold(dve, "scatter_add", n_items * 4)
        dve.sem_inc(sem("x_final"), 1)
        norm(3 * DEPTH + 1, x)

    @block.tensor
    def _(pe):
        def passes(out, hi_l, lo_l, hi_r, lo_r, start, stop):
            pe.matmul(out, hi_l, hi_r, start=start, stop=False, skip_group_check=True)
            pe.matmul(out, hi_l, lo_r, start=False, stop=False, skip_group_check=True)
            return pe.matmul(out, lo_l, hi_r, start=False, stop=stop, skip_group_check=True)

        def halves(st, u, which=(0, 1)):
            for half in which:
                pe.wait_ge(sem("raw_free"), st.upto(u, half) + 2 * RAW)
                yield half, w_hi[:, u % SPLIT, half, :], w_lo[:, u % SPLIT, half, :]

        def tokens_out(st, u, kn, width, xs, banks, first, last):
            x_hi, x_lo, k_x = xs
            n = kn // 2
            for half, h, lo_ in halves(st, u):
                for t, b in enumerate(banks):
                    for k in range(n):
                        s, r = slice(k * width, (k + 1) * width), slice(t * P, (t + 1) * P)
                        kx = k_x + half * n + k
                        mm = passes(bank[b][:, 0:width], x_hi[:, kx, r], x_lo[:, kx, r], h[:, s], lo_[:, s],
                                    first and half == 0 and k == 0, last and half == 1 and k == n - 1)
                mm.then_inc(sem("unit_used"), 1)

        def features_out(st, u, k0, xs, banks, first, last, which=(0, 1)):
            x_hi, x_lo = xs
            for half, h, lo_ in halves(st, u, which):
                for cb in range(4):
                    out = bank[banks[cb // 2]][:, (cb % 2) * T:(cb % 2) * T + T]
                    for k in range(2):
                        s, kx = slice(k * 512 + cb * P, k * 512 + (cb + 1) * P), k0 + 2 * half + k
                        mm = passes(out, h[:, s], lo_[:, s], x_hi[:, kx, :], x_lo[:, kx, :],
                                    first and half == 0 and k == 0 and cb % 2 == 0, last and half == 1 and k == 1)
                mm.then_inc(sem("unit_used"), 1)

        def norm(m, banks):
            for t in range(NT):
                pe.wait_ge(sem("xn_ready"), m * NT + t + 1)
                for half in range(2):
                    for k in range(4):
                        a = (4 * half + k) * P
                        mm = pe.transpose(bank[banks[2 * t + half]][:, k * P:(k + 1) * P], xn[:, t, a:a + P], ident)
                    mm.then_inc(sem("xT_mm"), 1)

        pe.sem_inc(sem("scatter_mm"), 4)
        pe.sem_inc(sem("unit_used"), 2 * SPLIT)
        pe.wait_ge(sem("mats_in"), 16)
        pe.wait_ge(sem("zeros"), 1)
        norm(0, (0, 1, 2, 3))
        pe.wait_ge(sem("table_in"), 32)
        pe.matmul(bank[7][0:HEADS, 0:SKEW_W], rel[:, :], table, start=True, stop=True).then_inc(sem("skew_mm"), 1)

        with pe.Fori(0, DEPTH) as l:
            l1 = l + 1
            st = Stream(l * (LAYER_UNITS + DENSE_UNITS), l * ((LAYER_UNITS + DENSE_UNITS) // RAW))
            xs = (xT_hi, xT_lo)
            pe.wait_ge(sem("xT_lo"), l * 16 + 3)
            features_out(st, 0, 0, xs, (4, 5), True, False)
            pe.wait_ge(sem("xT_lo"), l * 16 + 4)
            features_out(st, 1, 4, xs, (4, 5), False, True)
            pe.wait_ge(sem("skew_rows"), 1)
            features_out(st, 2, 0, xs, (6, 7), True, False)
            features_out(st, 3, 4, xs, (6, 7), False, True)
            tokens_out(st, 4, 4, 512, (xT_hi, xT_lo, 0), (0, 1), True, False)
            pe.wait_ge(sem("q_sb"), l1 * 2)
            pe.wait_ge(sem("k_sb"), l1 * 2)
            with pe.If(l < 1):
                norm(1, (4, 5, 6, 7))
            tokens_out(st, 5, 4, 512, (xT_hi, xT_lo, 4), (0, 1), False, True)
            pe.wait_ge(sem("xT_lo"), 8)
            for i in range(HEADS + 2):
                if i < HEADS:
                    h = i
                    if h >= 2:
                        pe.wait_ge(sem("logits"), l * HEADS + h - 1)
                    r = slice((h % 2) * 64, (h % 2) * 64 + 64)
                    pe.matmul(bank[6 + h % 2][:, 0:P], qk[r, 0, h // 2, 0:P], qk[r, 1, h // 2, 0:P],
                              start=True, stop=True)
                    pe.matmul(bank[6 + h % 2][:, P:3 * P], qk[r, 0, h // 2, P:T], qk[r, 1, h // 2, :],
                              start=True, stop=True).then_inc(sem("logits_mm"), 1)
                if 1 <= i <= HEADS:
                    h = i - 1
                    pe.wait_ge(sem("exp"), (l * HEADS + h + 1) * 2)
                    if h == 0:
                        pe.wait_ge(sem("v_sb"), l1 * 2)
                    if h >= 2:
                        pe.wait_ge(sem("probT_sb"), l * HEADS + h - 1)
                    for b in range(3):
                        mm = pe.transpose(bank[h % 2][:, b * P:(b + 1) * P], prob[:, h % 2, b * P:(b + 1) * P], ident)
                    mm.then_inc(sem("probT_mm"), 1)
                if i >= 2:
                    h = i - 2
                    pe.wait_ge(sem("probT_sb"), l * HEADS + h + 1)
                    d = slice(h * DH, (h + 1) * DH)
                    pe.matmul(bank[4][:, d], probT[:, h % 2, 0:P], v[:, 0, d], start=True, stop=True)
                    pe.matmul(bank[5][:, d], probT[:, h % 2, P:2 * P], v[:, 0, d], start=True, stop=False)
                    pe.matmul(bank[5][:, d], probT[:, h % 2, 2 * P:3 * P], v[:, 1, d], start=False, stop=True)\
                        .then_inc(sem("pv_mm"), 1)
                if i < 4:
                    features_out(st, 6 + i // 2, 4 * (i // 2), xs, (2, 3), i < 2, i >= 2, which=(i % 2,))
            pe.wait_ge(sem("logits"), l1 * HEADS)
            features_out(st, 8, 0, xs, (6, 7), True, False)
            for t in range(NT):
                pe.wait_ge(sem("y_tok"), l * 2 + t + 1)
                for k in range(4):
                    mm = pe.transpose(bank[4 + t][:, k * P:(k + 1) * P], y_tok[:, t, k * P:(k + 1) * P], ident)
                mm.then_inc(sem("yTok_mm"), 1)
            hold(pe, "params_in", l * 48 + 64)
            hold(pe, "pooled", l1)
            for b in range(2):
                for g in range(2):
                    r = slice(g * 64, g * 64 + 64)
                    mm = pe.matmul(bank[2][r, b * T:(b + 1) * T], pool_w[r, b, :], pooled[r, b, :],
                                   start=True, stop=True)
            mm.then_inc(sem("pool_mm"), 1)
            features_out(st, 9, 4, xs, (6, 7), False, True)
            pe.wait_ge(sem("yT_lo"), l * 5 + 2)
            tokens_out(st, 10, 4, 512, (yT_hi, yT_lo, 0), (0, 1), True, False)
            tokens_out(st, 11, 4, 512, (yT_hi, yT_lo, 0), (4, 5), True, False)
            pe.wait_ge(sem("yT_lo"), l * 5 + 5)
            tokens_out(st, 12, 4, 512, (yT_hi, yT_lo, 4), (0, 1), False, True)
            tokens_out(st, 13, 4, 512, (yT_hi, yT_lo, 4), (4, 5), False, True)
            ms = (memT_hi, memT_lo)
            features_out(st, 14, 0, ms, (6, 7), True, False)
            features_out(st, 15, 4, ms, (6, 7), False, True)
            norm(l * 3 + 2, (0, 1, 2, 3))
            tokens_out(st, 16, 4, 512, (memT_hi, memT_lo, 0), (4, 5), True, False)
            pe.wait_ge(sem("xT_lo"), l * 12 + 12)
            features_out(st, 17, 0, xs, (0, 1), True, False)
            features_out(st, 18, 4, xs, (0, 1), False, True)
            tokens_out(st, 19, 4, 512, (memT_hi, memT_lo, 4), (4, 5), False, True)
            pe.wait_ge(sem("xk_sb"), l1 * 2)
            pe.wait_ge(sem("xq_sb"), l1 * 2)
            for i in range(XHEADS + 2):
                if i < XHEADS:
                    h = i
                    if h >= 2:
                        pe.wait_ge(sem("xexp"), (l * XHEADS + h - 1) * 2)
                    for t in range(NT):
                        mm = pe.matmul(bank[2 + h % 2][:, t * T:(t + 1) * T], qk[:, 0, h, t * P:(t + 1) * P],
                                       qk[:, 1, h, :], start=True, stop=True)
                    mm.then_inc(sem("xlogits_mm"), 1)
                if 1 <= i <= XHEADS:
                    h = i - 1
                    pe.wait_ge(sem("xexp"), (l * XHEADS + h + 1) * 2)
                    if h >= 2:
                        pe.wait_ge(sem("xprobT_sb"), l * XHEADS + h - 1)
                    for b in range(4):
                        mm = pe.transpose(bank[h % 2][:, b * P:(b + 1) * P], prob[:, h % 2, b * P:(b + 1) * P], ident)
                    mm.then_inc(sem("xprobT_mm"), 1)
                if i >= 2:
                    h = i - 2
                    pe.wait_ge(sem("xprobT_sb"), l * XHEADS + h + 1)
                    if h == 0:
                        pe.wait_ge(sem("xv_sb"), l1 * 2)
                    d = slice(h * XDH, (h + 1) * XDH)
                    for t in range(NT):
                        for b in range(2):
                            a = (2 * t + b) * P
                            mm = pe.matmul(bank[6 + t][:, d], probT[:, h % 2, a:a + P], v[:, b, d],
                                           start=(b == 0), stop=(b == 1))
                    mm.then_inc(sem("xpv_mm"), 1)
            for t in range(NT):
                pe.wait_ge(sem("xy_tok"), l * 2 + t + 1)
                for k in range(4):
                    mm = pe.transpose(bank[4 + t][:, k * P:(k + 1) * P], y_tok[:, t, k * P:(k + 1) * P], ident)
                mm.then_inc(sem("xyT_mm"), 1)
            pe.wait_ge(sem("xyT_lo"), l1 * 2)
            for n in range(4):
                tokens_out(st, 20 + n, 2, 512, (yT_hi, yT_lo, 2 * (n % 2)), (2 * (n // 2), 2 * (n // 2) + 1),
                           n % 2 == 0, n % 2 == 1)
            norm(l * 3 + 3, (4, 5, 6, 7))
            pe.wait_ge(sem("xT_lo"), l * 12 + 15)

            def up(st, u, between, width, xs, banks):
                for m in range(2):
                    if m == 1 and between is not None:
                        between()
                    tokens_out(st, u + m, 4, width, (xs[0], xs[1], 4 * m), banks, m == 0, m == 1)

            def turn(width, tiles):
                for t in range(tiles):
                    for k in range(width // P):
                        mm = pe.transpose(bank[2 + t][:, k * P:(k + 1) * P], hid[:, t, k * P:(k + 1) * P], ident)
                mm.then_inc(sem("hidT_mm"), 1)

            def down(st, u, tiles, short=False, last=False):
                for m in range(2):
                    for half, h, lo_ in halves(st, u + m):
                        k = m if short else 2 * m + half
                        for t in range(tiles):
                            r = slice(t * P, (t + 1) * P)
                            for col in ((half,) if short else (0, 1)):
                                s = slice(0, 512) if short else slice(col * 512, (col + 1) * 512)
                                b = bank[4 + (2 * col + t if tiles == 2 else col)]
                                mm = passes(b[:, :], yT_hi[:, k, r], yT_lo[:, k, r], h[:, s], lo_[:, s],
                                            False, last and m == 1 and (short or half == 1))
                        mm.then_inc(sem("unit_used"), 1)

            def clear(banks):
                for b in banks:
                    pe.matmul(bank[b][:, :], zeros[:, 0:P], zeros[:, :], start=True, stop=False, skip_group_check=True)

            with pe.If(l < 1):
                st = Stream(LAYER_UNITS, LAYER_UNITS // RAW)
                up(st, 0, lambda: pe.wait_ge(sem("xT_lo"), 16), FT, xs, (0, 1))
                up(st, 2, None, FT, xs, (2, 3))
                clear((4, 5, 6, 7))
                with pe.Fori(1, DENSE_STEPS) as j:
                    sj = Stream(LAYER_UNITS + (j - 1) * 6, LAYER_UNITS // RAW + (j - 1))
                    pe.wait_ge(sem("hid_ready"), j * NT)
                    up(sj, 4, lambda: turn(FT, NT), FT, xs, (0, 1))
                    pe.wait_ge(sem("hidT_lo"), j * NT)
                    up(sj, 6, None, FT, xs, (2, 3))
                    down(sj, 8, NT)
                e = 4 + 6 * (DENSE_STEPS - 1)
                pe.wait_ge(sem("hid_ready"), DENSE_STEPS * NT)
                up(st, e, lambda: turn(FT, NT), FT // 2, xs, (0, 1))
                pe.wait_ge(sem("hidT_lo"), DENSE_STEPS * NT)
                up(st, e + 2, None, FT // 2, xs, (2, 3))
                down(st, e + 4, NT)
                pe.wait_ge(sem("hid_ready"), (DENSE_STEPS + 1) * NT)
                turn(FT // 2, NT)
                pe.wait_ge(sem("hidT_lo"), (DENSE_STEPS + 1) * NT)
                down(st, e + 6, NT, short=True, last=True)
                norm(4, (0, 1, 2, 3))
            pe.nop()

        pe.wait_ge(sem("xT_lo"), 16 * DEPTH - 4)
        pe.wait_ge(sem("router_lo"), 1)
        for k in range(KD):
            for part in (xT_hi, xT_lo):
                mm = pe.matmul(bank[0][0:2 * NE, 0:T], router_parts[:, k, :], part[:, k, :],
                               start=(k == 0 and part is xT_hi), stop=(k == KD - 1 and part is xT_lo))
        mm.then_inc(sem("router_mm"), 1)
        pe.wait_ge(sem("parts_sb"), 1)
        for t in range(NT):
            mm = pe.transpose(bank[2][:, t * 2 * NE:(t + 1) * 2 * NE], parts_sb[:, t * P:(t + 1) * P],
                              ident[0:2 * NE, 0:2 * NE])
        mm.then_inc(sem("parts_mm"), 1)
        pe.wait_ge(sem("mask"), 1)
        pe.matmul(bank[1][:, 0:NE], before, mask[:, 0, :], start=True, stop=True)
        pe.matmul(bank[1][:, NE:2 * NE], ones, mask[:, 0, :], start=True, stop=False)
        pe.matmul(bank[1][:, NE:2 * NE], before, mask[:, 1, :], start=False, stop=True)
        pe.matmul(bank[1][:, 2 * NE:3 * NE], ones, mask[:, 0, :], start=True, stop=False)
        pe.matmul(bank[1][:, 2 * NE:3 * NE], ones, mask[:, 1, :], start=False, stop=True).then_inc(sem("rank_mm"), 1)
        def gather(i):
            pe.wait_ge(sem("select"), i + 1)
            for b in range(2):
                for k in range(4):
                    a = (4 * b + k) * P
                    for t in range(NT):
                        mm = pe.matmul(bank[6 + b][:, k * P:(k + 1) * P], xn[:, t, a:a + P], S[:, t, :],
                                       start=(t == 0), stop=(t == NT - 1))
                mm.then_inc(sem("gather_mm"), 1)

        def scatter(i):
            pe.wait_ge(sem("rows_sb"), i * 2 + 2)
            pe.wait_ge(sem("SgT"), i + 1)
            for n in range(4):
                t, col = n // 2, n % 2
                pe.matmul(bank[SCATTER[n]][:, :], SgT[:, t, :], y_sb[:, col * 512:(col + 1) * 512],
                          start=True, stop=True).then_inc(sem("scatter_mm"), 1)

        gather(0)
        pe.wait_ge(sem("info_ready"), 1)
        n_items = pe.value_load(info[0:1, 0:1], min_val=NE, max_val=ITEMS)
        gs = (xgT_hi, xgT_lo)
        with pe.Fori(0, ITEMS) as i:
            with pe.If(n_items > i):
                st = Stream(i * ITEM_UNITS + MOE_BASE, i * (ITEM_UNITS // RAW) + MOE_BASE // RAW)
                pe.wait_ge(sem("gather_lo"), i * 2 + 2)
                up(st, 0, None, FT, gs, (0,))
                up(st, 2, None, FT, gs, (2,))
                with pe.If(i > 0):
                    scatter(i)
                clear((4, 5))
                with pe.Fori(1, ITEM_STEPS) as j:
                    sj = Stream(i * ITEM_UNITS + (j - 1) * 6 + MOE_BASE,
                                i * (ITEM_UNITS // RAW) + (j - 1) + MOE_BASE // RAW)
                    pe.wait_ge(sem("hid_ready"), i * ITEM_STEPS + j + NT * DENSE_TURNS)
                    up(sj, 4, lambda: turn(FT, 1), FT, gs, (0,))
                    pe.wait_ge(sem("hidT_lo"), i * ITEM_STEPS + j + NT * DENSE_TURNS)
                    up(sj, 6, None, FT, gs, (2,))
                    down(sj, 8, 1)
                pe.wait_ge(sem("hid_ready"), i * ITEM_STEPS + ITEM_STEPS + NT * DENSE_TURNS)
                turn(FT, 1)
                pe.wait_ge(sem("select_gated"), i + 1)
                for t in range(NT):
                    mm = pe.transpose(bank[1][:, t * P:(t + 1) * P], Sg[:, t, :], ident)
                mm.then_inc(sem("select_mm"), 1)
                gather(i + 1)
                pe.wait_ge(sem("hidT_lo"), i * ITEM_STEPS + ITEM_STEPS + NT * DENSE_TURNS)
                down(st, 4 + 6 * (ITEM_STEPS - 1), 1, last=True)
            pe.nop()
        pe.wait_ge(sem("gather_lo"), n_items * 2 + 2)
        scatter(n_items)


_INPUTS = ("x", "mem", "rel_bias", "mem_norm_g", "mix_norm_g", "w_in", "conv_w", "pool_w", "pool_scale", "w_out",
           "xattn_norm_g", "wq_x", "wkv_x", "wo_x", "ffn_norm_g", "w13_dense", "w2_dense", "router_w", "w13_moe",
           "w2_moe", "final_norm_g")


def kernel(**inputs):
    import concourse.bacc as bacc
    from concourse.bass_utils import run_bass_kernel_spmd

    nc = bacc.Bacc("TRN2", target_bir_lowering=False, num_devices=1)
    arrays, io = {}, {}
    given = {name: np.ascontiguousarray(inputs[name]) for name in _INPUTS}
    given.update(shape_constants())
    for name, a in given.items():
        arrays[f"in_{name}"] = a
        io[name] = nc.dram_tensor(f"in_{name}", a.shape, mybir.dt.from_np(a.dtype), kind="ExternalInput").ap()
    io["out"] = nc.dram_tensor("out", (1, T, D), F32, kind="ExternalOutput").ap()
    build(nc, io)
    r = run_bass_kernel_spmd(nc, [arrays], core_ids=[0])
    return r.results[0]["out"]
```
